# Optimizing a Trainium2 kernel written in Bass

```python
import jax, jax.numpy as jnp
from jax import lax
import numpy as np

D_MODEL = 2048
BATCH = 1
SEQ = 256
DEPTH = 1

MIX_WIDTH = D_MODEL
ATTN_WIDTH = MIX_WIDTH // 2
N_ATTN_HEADS = 8
HEAD_DIM = ATTN_WIDTH // N_ATTN_HEADS
ROT_DIM = HEAD_DIM // 4
ROPE_THETA = 500000.0
MOBA_BLOCK = 256
MOBA_TOPK = 3
Q_CHUNK = 32
REC_WIDTH = MIX_WIDTH - ATTN_WIDTH
N_REC_BLOCKS = 16
REC_BLOCK_DIM = REC_WIDTH // N_REC_BLOCKS
CONV_WIDTH = 4
RGLRU_C = 8.0
IN_COLS = 3 * ATTN_WIDTH + 2 * REC_WIDTH
D_FF = ((8 * D_MODEL // 3 + 127) // 128) * 128
FFN_HALF = 0.5
EPS = 1e-6

kernel_name = "macaron_moba_rglru_hybrid_layer"

def rms_norm(x, g):
    x32 = x.astype(jnp.float32)
    y = x32 * lax.rsqrt(jnp.mean(x32 * x32, axis=-1, keepdims=True) + EPS)
    return (y * g.astype(jnp.float32)).astype(x.dtype)

def swiglu(h, w_gate_up, w_down):
    gu = h @ w_gate_up
    g, u = jnp.split(gu, 2, axis=-1)
    return (jax.nn.silu(g) * u) @ w_down

def partial_rope(x, pos):
    inv_freq = ROPE_THETA ** (-jnp.arange(0, ROT_DIM, 2, dtype=jnp.float32) / ROT_DIM)
    ang = pos.astype(jnp.float32)[:, None] * inv_freq[None, :]
    cos, sin = jnp.cos(ang), jnp.sin(ang)
    xr = x[..., :ROT_DIM].astype(jnp.float32)
    x1, x2 = jnp.split(xr, 2, axis=-1)
    rot = jnp.concatenate([x1 * cos - x2 * sin, x2 * cos + x1 * sin], axis=-1)
    return jnp.concatenate([rot.astype(x.dtype), x[..., ROT_DIM:]], axis=-1)

def moba_attention(q, k, v):
    B, H, S, hd = q.shape
    nb = -(-S // MOBA_BLOCK)
    pad = nb * MOBA_BLOCK - S
    kp = jnp.pad(k, ((0, 0), (0, 0), (0, pad), (0, 0)))
    vp = jnp.pad(v, ((0, 0), (0, 0), (0, pad), (0, 0)))
    kb = kp.reshape(B, H, nb, MOBA_BLOCK, hd)
    vb = vp.reshape(B, H, nb, MOBA_BLOCK, hd)
    kmean = jnp.mean(kb.astype(jnp.float32), axis=3)
    k_eff = min(MOBA_TOPK, nb)
    nc = S // Q_CHUNK
    qc = q.reshape(B, H, nc, Q_CHUNK, hd).transpose(2, 0, 1, 3, 4)
    scale = HEAD_DIM ** -0.5
    bi = jnp.arange(B)[:, None, None, None]
    hi = jnp.arange(H)[None, :, None, None]
    blk_ids = jnp.arange(nb)

    def one_chunk(args):
        q_c, c = args
        own = (c * Q_CHUNK) // MOBA_BLOCK
        q_pos = c * Q_CHUNK + jnp.arange(Q_CHUNK)
        q32 = q_c.astype(jnp.float32)
        gate = jnp.einsum('bhqd,bhnd->bhqn', q32, kmean)
        gate = jnp.where(blk_ids < own, gate, -jnp.inf)
        _, sel = lax.top_k(gate, k_eff)
        sel_valid = jnp.arange(k_eff) < own
        k_sel = kb[bi, hi, sel]
        v_sel = vb[bi, hi, sel]
        s_sel = jnp.einsum('bhqd,bhqnkd->bhqnk', q_c, k_sel).astype(jnp.float32) * scale
        s_sel = jnp.where(sel_valid[:, None], s_sel, -jnp.inf)
        s_sel = s_sel.reshape(B, H, Q_CHUNK, k_eff * MOBA_BLOCK)
        k_own = lax.dynamic_index_in_dim(kb, own, axis=2, keepdims=False)
        v_own = lax.dynamic_index_in_dim(vb, own, axis=2, keepdims=False)
        s_own = jnp.einsum('bhqd,bhkd->bhqk', q_c, k_own).astype(jnp.float32) * scale
        key_pos = own * MOBA_BLOCK + jnp.arange(MOBA_BLOCK)
        s_own = jnp.where(key_pos[None, :] <= q_pos[:, None], s_own, -jnp.inf)
        p = jax.nn.softmax(jnp.concatenate([s_sel, s_own], axis=-1), axis=-1)
        p_sel = p[..., :k_eff * MOBA_BLOCK].reshape(B, H, Q_CHUNK, k_eff, MOBA_BLOCK).astype(v.dtype)
        p_own = p[..., k_eff * MOBA_BLOCK:].astype(v.dtype)
        return (jnp.einsum('bhqnk,bhqnkd->bhqd', p_sel, v_sel)
                + jnp.einsum('bhqk,bhkd->bhqd', p_own, v_own))

    out = lax.map(one_chunk, (qc, jnp.arange(nc)))
    return out.transpose(1, 2, 0, 3, 4).reshape(B, H, S, hd)

def causal_depthwise_conv(x, w, b):
    y = lax.conv_general_dilated(
        x, w[:, None, :].astype(x.dtype), window_strides=(1,),
        padding=[(CONV_WIDTH - 1, 0)], dimension_numbers=('NWC', 'WIO', 'NWC'),
        feature_group_count=x.shape[-1])
    return y + b

def rg_lru(x, w_a, b_a, w_x, b_x, lam):
    B, S, R = x.shape
    xb = x.reshape(B, S, N_REC_BLOCKS, REC_BLOCK_DIM)
    r = jax.nn.sigmoid(jnp.einsum('bsni,nij->bsnj', xb, w_a).reshape(B, S, R) + b_a)
    i = jax.nn.sigmoid(jnp.einsum('bsni,nij->bsnj', xb, w_x).reshape(B, S, R) + b_x)
    log_a = (-RGLRU_C * r.astype(jnp.float32)) * jax.nn.softplus(-lam.astype(jnp.float32))
    a = jnp.exp(log_a)
    mult = jnp.sqrt(-jnp.expm1(2.0 * log_a))
    u = mult * (i * x).astype(jnp.float32)

    def combine(c1, c2):
        a1, b1 = c1
        a2, b2 = c2
        return a1 * a2, a2 * b1 + b2

    _, h = lax.associative_scan(combine, (a, u), axis=1)
    return h.astype(x.dtype)

def setup_inputs(seed: int = 0) -> dict:
    key = jax.random.key(seed)
    ks = jax.random.split(key, 32)
    f32 = jnp.float32
    L = DEPTH

    def nrm(k, shape, scale):
        return jax.random.normal(k, shape, f32) * scale

    def gain(k, n):
        return 1.0 + 0.05 * jax.random.normal(k, (L, n), f32)

    a0 = jax.random.uniform(ks[13], (L, REC_WIDTH), f32, 0.9, 0.999)
    return {
        "x": nrm(ks[0], (BATCH, SEQ, D_MODEL), 1.0),
        "ffn1_pre_g": gain(ks[1], D_MODEL),
        "ffn1_w_gate_up": nrm(ks[2], (L, D_MODEL, 2 * D_FF), D_MODEL ** -0.5),
        "ffn1_w_down": nrm(ks[3], (L, D_FF, D_MODEL), D_FF ** -0.5),
        "ffn1_post_g": gain(ks[4], D_MODEL),
        "mix_pre_g": gain(ks[5], D_MODEL),
        "w_in": nrm(ks[6], (L, D_MODEL, IN_COLS), D_MODEL ** -0.5),
        "conv_w": nrm(ks[7], (L, CONV_WIDTH, REC_WIDTH), CONV_WIDTH ** -0.5),
        "conv_b": nrm(ks[8], (L, REC_WIDTH), 0.01),
        "rg_w_a": nrm(ks[9], (L, N_REC_BLOCKS, REC_BLOCK_DIM, REC_BLOCK_DIM), REC_BLOCK_DIM ** -0.5),
        "rg_b_a": nrm(ks[10], (L, REC_WIDTH), 0.01),
        "rg_w_x": nrm(ks[11], (L, N_REC_BLOCKS, REC_BLOCK_DIM, REC_BLOCK_DIM), REC_BLOCK_DIM ** -0.5),
        "rg_b_x": nrm(ks[12], (L, REC_WIDTH), 0.01),
        "rg_lambda": jnp.log(a0) - jnp.log1p(-a0),
        "attn_out_g": gain(ks[14], ATTN_WIDTH),
        "rec_out_g": gain(ks[15], REC_WIDTH),
        "w_out": nrm(ks[16], (L, MIX_WIDTH, D_MODEL), MIX_WIDTH ** -0.5),
        "mix_post_g": gain(ks[17], D_MODEL),
        "ffn2_pre_g": gain(ks[18], D_MODEL),
        "ffn2_w_gate_up": nrm(ks[19], (L, D_MODEL, 2 * D_FF), D_MODEL ** -0.5),
        "ffn2_w_down": nrm(ks[20], (L, D_FF, D_MODEL), D_FF ** -0.5),
        "ffn2_post_g": gain(ks[21], D_MODEL),
    }

def reference(x, ffn1_pre_g, ffn1_w_gate_up, ffn1_w_down, ffn1_post_g,
              mix_pre_g, w_in, conv_w, conv_b, rg_w_a, rg_b_a, rg_w_x, rg_b_x,
              rg_lambda, attn_out_g, rec_out_g, w_out, mix_post_g,
              ffn2_pre_g, ffn2_w_gate_up, ffn2_w_down, ffn2_post_g):
    B, S, _ = x.shape
    pos = jnp.arange(S, dtype=jnp.int32)
    splits = [ATTN_WIDTH, 2 * ATTN_WIDTH, 3 * ATTN_WIDTH, 3 * ATTN_WIDTH + REC_WIDTH]

    def heads(t):
        return t.reshape(B, S, N_ATTN_HEADS, HEAD_DIM).transpose(0, 2, 1, 3)

    for l in range(DEPTH):
        f = swiglu(rms_norm(x, ffn1_pre_g[l]), ffn1_w_gate_up[l], ffn1_w_down[l])
        x = x + FFN_HALF * rms_norm(f, ffn1_post_g[l])

        h = rms_norm(x, mix_pre_g[l])
        proj = h @ w_in[l]
        q, k, v, xr, gr = jnp.split(proj, splits, axis=-1)
        q = partial_rope(heads(q), pos)
        k = partial_rope(heads(k), pos)
        attn = moba_attention(q, k, heads(v))
        attn = attn.transpose(0, 2, 1, 3).reshape(B, S, ATTN_WIDTH)
        xc = causal_depthwise_conv(xr, conv_w[l], conv_b[l])
        rec = rg_lru(xc, rg_w_a[l], rg_b_a[l], rg_w_x[l], rg_b_x[l], rg_lambda[l])
        rec = rec * jax.nn.gelu(gr)
        merged = jnp.concatenate([rms_norm(attn, attn_out_g[l]),
                                  rms_norm(rec, rec_out_g[l])], axis=-1)
        y = merged @ w_out[l]
        x = x + rms_norm(y, mix_post_g[l])

        f = swiglu(rms_norm(x, ffn2_pre_g[l]), ffn2_w_gate_up[l], ffn2_w_down[l])
        x = x + FFN_HALF * rms_norm(f, ffn2_post_g[l])
    return x


_drawn_inputs = setup_inputs


def setup_inputs(seed=0):
    import zlib

    import numpy as np

    out = dict(_drawn_inputs(seed))
    spreads = {}
    factors = {'conv_b': 3.109, 'rg_b_a': 42.243, 'rg_b_x': 26.089, 'ffn2_post_g': 3.493}
    for name, (base, spread) in spreads.items():
        noise = np.random.default_rng([zlib.crc32(name.encode()), seed]).standard_normal(out[name].shape)
        drawn = base * np.exp(spread * noise) if base else spread * noise
        out[name] = __import__('jax').numpy.asarray(drawn.astype(out[name].dtype))
    for name, factor in factors.items():
        out[name] = (out[name] * factor).astype(out[name].dtype)
    return out
```

```python
from contextlib import ExitStack

import numpy as np

import concourse.bass as bass
from concourse import mybir
from concourse.alu_op_type import AluOpType as ALU

ACT = mybir.ActivationFunctionType
AX = mybir.AxisListType
F32 = mybir.dt.float32
F32R = mybir.dt.float32r

P = 128
T = 256
D = 2048
KD = D // P
FF = ((8 * D // 3 + 127) // 128) * 128
KF = FF // P
HEADS = 8
REC_TILES = 8
PIECE = 8
DOWN_PIECES = -(-KF // PIECE)
SLOTS = 4
EPS = 1e-6
MASKED = -3.0e38
GELU_C = 0.044715
GELU_S = float(np.sqrt(2.0 / np.pi))

UP1, DOWN1, REC, ATT = 0, 4 * KF, 4 * KF + DOWN_PIECES * KD, 4 * KF + DOWN_PIECES * KD + 4 * REC_TILES
OUT = ATT + 6 * HEADS
UP2 = OUT + 2 * KD
DOWN2 = UP2 + 4 * KF
END = DOWN2 + DOWN_PIECES * KD
G_UP1, G_DOWN1 = 0, KF
G_REC = G_DOWN1 + KD
G_ATT = G_REC + REC_TILES
G_OUT = G_ATT + HEADS
G_UP2 = G_OUT + KD
G_DOWN2 = G_UP2 + KF
assert all(n % SLOTS == 0 for n in (DOWN1, REC, ATT, OUT, UP2, DOWN2, END))

C_FFN1_PRE, C_FFN1_POST, C_MIX_PRE, C_REC_OUT, C_ATT_OUT, C_MIX_POST, C_FFN2_PRE, C_FFN2_POST = (
    0, 16, 32, 48, 56, 64, 80, 96)
C_CONV_W, C_CONV_B, C_BA, C_BX, C_LAM, C_EPS = 112, 144, 152, 160, 168, 176
N_PARAM = 178


def tiles(eng, count, peel, unroll):
    for n in range(peel):
        yield n, n
    rounds = (count - peel) // unroll
    if rounds:
        with eng.Fori(0, rounds) as i:
            for r in range(unroll):
                yield i * unroll + (peel + r), peel + r
    for n in range(peel + rounds * unroll, count):
        yield n, n


def layer(nc, x, up1, down1, rec_in, att_in, out_w, up2, down2, params, gates, rope, consts, y):
    with ExitStack() as ctx:
        def sem(name):
            return ctx.enter_context(nc.semaphore(name))

        top = [(nc.sbuf_base + 63) // 64 * 64]

        def place(name, shape, dtype=F32, at=None):
            size = -(-4 * int(np.prod(shape[1:])) // 32) * 32
            offset = top[0] if at is None else at[0]
            if at is None:
                top[0] += size
            else:
                at[0] += size
            return nc.alloc_sbuf_tensor_at(name, shape, dtype, offset=offset)

        raw = place("weights_raw", [P, SLOTS, PIECE * P])
        w_hi = place("weights_hi", [P, SLOTS, PIECE * P], F32R)
        w_lo = place("weights_lo", [P, SLOTS, PIECE * P], F32R)
        xs = place("x_residual", [P, KD, T])
        operand = place("operand_hi_lo", [P, KD, 2 * T], F32R)
        param = place("channel_params", [P, N_PARAM])
        ones = place("ones", [P, P])
        pre_scale = place("pre_scale", [P, T])
        post_scale = place("post_scale", [P, T])
        scratch = place("scratch", [P, 6 * T])
        f_base = top[0]
        f = place("f", [P, KD, T])
        hidden_base = top[0]
        hidden = place("hidden_hi_lo", [P, KF, 2 * T], F32R)
        hidden_end = top[0]
        assert hidden_end <= nc.sbuf_usable_end

        at = [f_base]
        gate_w = place("gate_weights", [P, REC_TILES, 2, P], at=at)
        mask = place("causal_mask", [P, 3 * P], at=at)
        ident = place("identity", [P, P], at=at)
        rope_t = place("rope_tables", [32, 2, T], at=at)
        rope_tmp = place("rope_tmp", [32, 2, T], at=at)
        v_rows = place("v_rows", [P, 2, P], at=at)
        assert at[0] <= hidden_base

        at = [hidden_base]
        merged = place("merged_hi_lo", [P, KD, 2 * T], F32R, at=at)
        squares = place("squares", [P, KD, T], at=[hidden_base])
        decay = place("decay", [P, REC_TILES, T], at=at)
        tanh_la = place("tanh_half_log_a", [P, REC_TILES, T], at=at)
        gated_in = place("gated_in", [P, REC_TILES, T], at=at)
        gelu = place("gelu", [P, REC_TILES, T], at=at)
        att = place("attention_out", [P, HEADS, T], at=at)
        xg = place("xr_and_gr", [P, 2, T + 4], at=at)
        conv = place("conv_out", [P, 2, T], at=at)
        gelu_tmp = place("gelu_tmp", [P, T], at=at)
        gate_t = place("gate_tanh", [P, 2, T], at=at)
        q_rec = place("q_rec", [P, T], at=at)
        gate_w2 = place("gate_weights_now", [P, 2, 2, P], at=at)
        rec_sq = place("rec_square", [P, T], at=at)
        rec_const = place("rec_const", [P, 4, REC_TILES], at=at)
        soft = place("softplus_tmp", [P, 8, REC_TILES], at=at)
        stat = place("softmax_stats", [P, 8], at=at)
        assert at[0] <= hidden_end, (at[0], hidden_end)
        at = [hidden_base + 4 * KD * T]
        qkv = place("q_k_v", [P, 3, T], at=at)
        att_total = place("attention_squares", [P, T], at=at)
        banks = ctx.enter_context(nc.psum_tensor("banks", [P, 8, 512], F32))

        params_loaded, ones_set, mixer_loaded = sem("params_loaded"), sem("ones_set"), sem("mixer_loaded")
        x_loaded = [sem(f"x_loaded{i}") for i in range(4)]
        raw_loaded = [sem(f"raw_loaded{i}") for i in range(SLOTS)]
        hi_done, lo_done, piece_used = sem("hi_done"), sem("lo_done"), sem("piece_used")
        right_half, evacuated, scaled = sem("right_half"), sem("evacuated"), sem("scaled")
        silu_done, gated, h_hi, h_lo = sem("silu_done"), sem("gated"), sem("h_hi"), sem("h_lo")
        sq_done, sq_summed = sem("sq_done"), sem("sq_summed")
        norm_summed, norm_root, norm_ready = sem("norm_summed"), sem("norm_root"), sem("norm_ready")
        f_scaled, x_new, op_hi, op_lo = sem("f_scaled"), sem("x_new"), sem("op_hi"), sem("op_lo")
        x_squared, tree = sem("x_squared"), sem("tree")
        y_stored = sem("y_stored")
        pads_zero, conv0, conv_step, conv_done = sem("pads_zero"), sem("conv0"), sem("conv_step"), sem("conv_done")
        gr_squared, gelu_step, gelu_th, gelu_done = sem("gr_squared"), sem("gelu_step"), sem("gelu_th"), sem("gelu_done")
        gelu_mul, rec_den = sem("gelu_mul"), sem("rec_den")
        gatew_now, gates_done, gate_tanh, rec_step = sem("gatew_now"), sem("gates_done"), sem("gate_tanh"), sem("rec_step")
        soft_step, soft_act = sem("soft_step"), sem("soft_act")
        root_t, u_done, scan_step, rec_done = sem("root_t"), sem("u_done"), sem("scan_step"), sem("rec_done")
        rec_sqd, rec_sum = sem("rec_sqd"), sem("rec_sum")
        m_f, m_hi, m_lo = sem("m_f"), sem("m_hi"), sem("m_lo")
        rope_step, scored, softmax_step, exp_done = (
            sem("rope_step"), sem("scored"), sem("softmax_step"), sem("exp_done"))
        v_turned, v_copied, p_ready, p_turned, p_copied = (
            sem("v_turned"), sem("v_copied"), sem("p_ready"), sem("p_turned"), sem("p_copied"))
        pv_done, att_copied, att_sqd, att_sum = sem("pv_done"), sem("att_copied"), sem("att_sqd"), sem("att_sum")

        t2 = scratch[:, 0:2 * T].rearrange("p (i t) -> p i t", i=2)
        gu = scratch[:, 2 * T:4 * T].rearrange("p (i t) -> p i t", i=2)
        sg = scratch[:, 4 * T:5 * T]
        sq = scratch[:, 5 * T:6 * T]
        t3 = scratch[:, 0:3 * T].rearrange("p (i t) -> p i t", i=3)
        prob = scratch[:, 3 * T:3 * T + 3 * P]
        prob_t = scratch[:, 3 * T + 3 * P:3 * T + 6 * P]

        def both(ap, n=2):
            return ap.unsqueeze(1).to_broadcast([ap.shape[0], n, T])

        def size_of(n_static):
            for first in (DOWN1, DOWN2):
                if first <= n_static < first + DOWN_PIECES * KD:
                    j = (n_static - first) % DOWN_PIECES
                    return P * (min(KF, PIECE * (j + 1)) - PIECE * j)
            return P * PIECE

        block = ctx.enter_context(nc.Block())

        @block.sync
        def _(sp):
            def load(n, s, src):
                if s >= SLOTS:
                    sp.wait_ge(lo_done, n - (SLOTS - 1))
                sp.dma_start(raw[:, s % SLOTS, 0:size_of(s)], src).then_inc(raw_loaded[s % SLOTS], 16)

            def load_groups(w, base, count, per, peel, unroll, after_first=None):
                for g, s in tiles(sp, count, peel, unroll):
                    for kh in range(2):
                        for i in range(per):
                            j = kh * per + i
                            src = w[bass.ds(g * per + i, 1), :, kh * PIECE * P:(kh + 1) * PIECE * P]
                            load(g * (2 * per) + (base + j), s * 2 * per + base + j,
                                 src.rearrange("a p c -> p (a c)"))
                    if s == 0 and after_first is not None:
                        after_first()

            def load_down(w, base):
                for d, s in tiles(sp, KD, 0, 2):
                    for j in range(DOWN_PIECES):
                        a = base + s * DOWN_PIECES + j
                        src = w[bass.ds(d, 1), :, j * PIECE * P:j * PIECE * P + size_of(a)]
                        load(d * DOWN_PIECES + (base + j), a, src.rearrange("a p c -> p (a c)"))

            def mixer_tables():
                sp.wait_ge(pads_zero, 2)
                for half in range(2):
                    rows = slice(64 * half, 64 * half + 64)
                    for g in range(2):
                        sp.dma_start(gate_w[rows, :, g, 64 * half:64 * half + 64], gates[g, half])\
                            .then_inc(mixer_loaded, 16)
                sp.dma_start(mask[:, :], consts[:, 0:3 * P]).then_inc(mixer_loaded, 16)
                sp.dma_start(ident[:, :], consts[:, 3 * P:4 * P]).then_inc(mixer_loaded, 16)
                sp.dma_start(rope_t[:, :, :], rope).then_inc(mixer_loaded, 16)

            sp.dma_start(param[:, :], params).then_inc(params_loaded, 16)
            for c in range(4):
                sp.dma_start(xs[:, 4 * c:4 * c + 4, :], x[:, 4 * c:4 * c + 4, :]).then_inc(x_loaded[c], 16)
            load_groups(up1, UP1, KF, 2, 1, 2)
            load_down(down1, DOWN1)
            load_groups(rec_in, REC, REC_TILES, 2, 2, 2, mixer_tables)
            load_groups(att_in, ATT, HEADS, 3, 0, 2)
            load_groups(out_w, OUT, KD // 4, 4, 0, 1)
            load_groups(up2, UP2, KF, 2, 0, 2)
            load_down(down2, DOWN2)
            for k in range(KD):
                sp.wait_ge(x_new, 2 * KD + k + 1)
                sp.dma_start(y[:, k, :], xs[:, k, :]).then_inc(y_stored, 16)
            sp.wait_ge(y_stored, 16 * KD)

        @block.tensor
        def _(pe):
            def piece(n, s, bank, k0, moving, first, last, k_ready=None):
                pe.wait_ge(lo_done, n + 1)
                for kk in range(size_of(s) // P):
                    k = k0 + kk
                    if k_ready is not None:
                        k_ready(k)
                    cols = slice(kk * P, (kk + 1) * P)
                    nc.tensor.matmul(banks[:, bank, :], w_hi[:, s % SLOTS, cols], moving[:, k, :],
                                     start=first and kk == 0, stop=False)
                    mm = nc.tensor.matmul(banks[:, bank, 0:T], w_lo[:, s % SLOTS, cols], moving[:, k, 0:T],
                                          start=False, stop=last and kk == size_of(s) // P - 1)
                mm.then_inc(piece_used, 1)
                return mm

            def group(g, s, base, per, bank_of, k_ready=None, between=None):
                for kh in range(2):
                    for i in range(per):
                        j = kh * per + i
                        mm = piece(g * (2 * per) + (base + j), s * 2 * per + base + j, bank_of(i),
                                   kh * PIECE, operand, kh == 0, kh == 1,
                                   k_ready if i == 0 else None)
                    if kh == 0 and between is not None:
                        between()
                return mm

            def token_sums(values, m, wait_sem, wait_value):
                pe.wait_ge(wait_sem, wait_value)
                nc.tensor.matmul(banks[:, 5, 0:T], ones[:, :], values, start=True, stop=True).then_inc(norm_summed, 1)

            def ffn(up_base, down_base, g_up, g_down, m, n_op, n_h):
                for g, s in tiles(pe, KF, 2, 2):
                    if s == 0:
                        ready = lambda k: pe.wait_ge(op_lo, n_op + k + 1)
                    else:
                        ready = None
                    if s >= 2:
                        pe.wait_ge(evacuated, g + (g_up - 1))
                    group(g, s, up_base, 2, lambda i: 2 * (s % 2) + i, ready)
                    if s == 0:
                        token_sums(squares[:, 0, :], m, tree, 4 if m == 0 else 12)
                for d, s in tiles(pe, KD, 4, 4):
                    if s < 2:
                        pe.wait_ge(evacuated, g_up + KF - 1)
                    elif s < 4:
                        pe.wait_ge(evacuated, g_up + KF)
                    else:
                        pe.wait_ge(evacuated, d + (g_down - 3))
                    for j in range(DOWN_PIECES):
                        a = down_base + s * DOWN_PIECES + j
                        ready = (lambda k: pe.wait_ge(h_lo, n_h + k + 1)) if s == 0 else None
                        mm = piece(d * DOWN_PIECES + (down_base + j), a, (s + 2) % 4, PIECE * j, hidden,
                                   j == 0, j == DOWN_PIECES - 1, ready)
                token_sums(post_scale[:, :], m + 1, sq_summed, KD * (1 if m == 0 else 3))

            pe.wait_ge(ones_set, 1)
            ffn(UP1, DOWN1, G_UP1, G_DOWN1, 0, 0, 0)

            def gate_products(n, s):
                pe.wait_ge(conv_done, n + 1)
                pe.wait_ge(gatew_now, n + 1)
                if s >= 1:
                    pe.wait_ge(gate_tanh, 3 * n)
                nc.tensor.matmul(banks[:, 6, 0:T], gate_w2[:, s % 2, 0, :], conv[:, s % 2, :], start=True, stop=True)
                nc.tensor.matmul(banks[:, 6, T:2 * T], gate_w2[:, s % 2, 1, :], conv[:, s % 2, :],
                                 start=True, stop=True).then_inc(gates_done, 1)

            for g, s in tiles(pe, REC_TILES, 4, 2):
                if s >= 2:
                    pe.wait_ge(evacuated, g + (G_REC - 1))
                ready = (lambda k: pe.wait_ge(op_lo, KD + k + 1)) if s == 0 else None
                group(g, s, REC, 2, lambda i: 2 * ((s + 1) % 2) + i, ready,
                           (lambda: gate_products(g - 2, s - 2)) if s >= 2 else None)
                if s == 0:
                    token_sums(squares[:, 0, :], 2, tree, 8)

            def scores(h, s):
                pe.wait_ge(rope_step, h * 4 + 4)
                if s >= 1:
                    pe.wait_ge(p_copied, h)
                    pe.wait_ge(v_copied, h)
                    pe.wait_ge(att_copied, h)
                else:
                    pe.wait_ge(gate_tanh, 3 * REC_TILES)
                q, k = qkv[:, 0, :], qkv[:, 1, :]
                nc.tensor.matmul(banks[:, 6, 0:P], q[:, 0:P], k[:, 0:P], start=True, stop=True)
                nc.tensor.matmul(banks[:, 6, P:2 * P], q[:, P:T], k[:, P:T], start=True, stop=True)
                nc.tensor.matmul(banks[:, 6, 2 * P:3 * P], q[:, P:T], k[:, 0:P], start=True, stop=True)\
                    .then_inc(scored, 1)
                pe.wait_ge(mixer_loaded, 7 * 16)
                nc.tensor.transpose(banks[:, 7, 0:P], qkv[:, 2, 0:P], ident[:, :])
                nc.tensor.transpose(banks[:, 7, P:2 * P], qkv[:, 2, P:T], ident[:, :]).then_inc(v_turned, 1)

            def turn_probs(h):
                pe.wait_ge(p_ready, h * 2 + 2)
                nc.tensor.transpose(banks[:, 6, 0:P], prob[:, 0:P], ident[:, :])
                nc.tensor.transpose(banks[:, 6, P:2 * P], prob[:, 2 * P:3 * P], ident[:, :])
                nc.tensor.transpose(banks[:, 6, 2 * P:3 * P], prob[:, P:2 * P], ident[:, :]).then_inc(p_turned, 1)

            def weighted_v(h, s):
                pe.wait_ge(v_copied, h + 1)
                if s >= 1:
                    pe.wait_ge(att_copied, h)
                pe.wait_ge(p_copied, h + 1)
                nc.tensor.matmul(banks[:, 7, T:2 * T], v_rows[:, 0, :], prob_t[:, 0:T], start=True, stop=False)
                nc.tensor.matmul(banks[:, 7, T + P:2 * T], v_rows[:, 1, :], prob_t[:, T:T + P],
                                 start=False, stop=True).then_inc(pv_done, 1)

            for h, s in tiles(pe, HEADS, 4, 2):
                b0 = 3 * ((s + 1) % 2)
                if s >= 1:
                    pe.wait_ge(evacuated, h + (G_ATT - 1))
                else:
                    pe.wait_ge(evacuated, G_ATT - 1)
                for j in range(6):
                    kh, i = divmod(j, 3)
                    mm = piece(h * 6 + (ATT + j), ATT + s * 6 + j, b0 + i, kh * PIECE, operand, kh == 0, kh == 1)
                    if s < 2 and j == 0:
                        gate_products(REC_TILES - 2 + s, REC_TILES - 2 + s)
                    if s >= 2 and j == 0:
                        weighted_v(h - 2, s - 2)
                    if s >= 1 and j == 2 and s != 1:
                        scores(h - 1, s - 1)
                    if s == 1 and j == 3:
                        scores(h - 1, s - 1)
                    if s >= 1 and j == 5:
                        turn_probs(h - 1)

            def out_piece(g, s, j, ready=None):
                kh, i = divmod(j, 4)
                if kh == 0 and s >= 1:
                    pe.wait_ge(evacuated, g * 4 + (G_OUT - 3 + i))
                piece(g * 8 + (OUT + j), OUT + s * 8 + j, i, kh * PIECE, merged, kh == 0, kh == 1, ready)

            last = HEADS - 1
            pe.wait_ge(evacuated, G_ATT + HEADS - 1)
            token_sums(post_scale[:, :], 3, rec_sum, REC_TILES)
            weighted_v(last - 1, last - 1)
            pe.wait_ge(evacuated, G_ATT + HEADS)
            scores(last, last)
            out_piece(0, 0, 0, lambda k: pe.wait_ge(m_lo, k + 1))
            out_piece(0, 0, 1)
            turn_probs(last)
            out_piece(0, 0, 2)
            weighted_v(last, last)
            out_piece(0, 0, 3)
            token_sums(pre_scale[:, :], 4, att_sum, HEADS)
            out_piece(0, 0, 4, lambda k: pe.wait_ge(m_lo, k + 1))
            for j in range(5, 8):
                out_piece(0, 0, j)
            for g, s in tiles(pe, KD // 4 - 1, 0, 1):
                for j in range(8):
                    out_piece(g + 1, s + 1, j)
            token_sums(post_scale[:, :], 5, sq_summed, 2 * KD)
            ffn(UP2, DOWN2, G_UP2, G_DOWN2, 6, 2 * KD, KF)

        @block.scalar
        def _(act):
            def split_hi(n, s):
                act.wait_ge(raw_loaded[s % SLOTS], n * 4 + (16 - 4 * (s % SLOTS)))
                if s >= SLOTS:
                    act.wait_ge(piece_used, n - (SLOTS - 1))
                cols = slice(0, size_of(s))
                nc.scalar.copy(w_hi[:, s % SLOTS, cols], raw[:, s % SLOTS, cols]).then_inc(hi_done, 1)

            def right(pieces, e, bank, n, dst):
                act.wait_ge(piece_used, pieces)
                act.wait_ge(evacuated, e)
                nc.scalar.copy(dst, banks[:, bank:bank + n, T:2 * T]).then_inc(right_half, 1)

            def silu(n, s, n_h):
                act.wait_ge(scaled, n + (1 + (0 if n_h == 0 else KF + REC_TILES + HEADS)))
                if s >= 1 or n_h:
                    act.wait_ge(h_lo, n + n_h)
                nc.scalar.activation(sg, gu[:, 0, :], ACT.Silu).then_inc(silu_done, 1)

            def hidden_hi(n, n_h):
                act.wait_ge(gated, n + (n_h + 1))
                nc.scalar.copy(hidden[:, bass.ds(n, 1), 0:T].rearrange("p a t -> p (a t)"), sg).then_inc(h_hi, 1)

            def root(m, dst, scale, eps_col):
                act.wait_ge(norm_summed, m + 1)
                nc.scalar.activation(dst, banks[:, 5, 0:T], ACT.Sqrt, bias=param[:, C_EPS + eps_col:C_EPS + eps_col + 1],
                                     scale=scale).then_inc(norm_root, 1)

            def square_f(d, s, e, n_sq):
                act.wait_ge(evacuated, e + 1)
                if s >= 1 or n_sq:
                    act.wait_ge(sq_summed, d + n_sq)
                nc.scalar.activation(sq, f[:, bass.ds(d, 1), :].rearrange("p a t -> p (a t)"),
                                     ACT.Square).then_inc(sq_done, 1)

            def operand_hi(n_op, gain, updated):
                for k in range(KD):
                    if updated is None:
                        if k % 4 == 0:
                            act.wait_ge(x_loaded[k // 4], 16)
                    else:
                        act.wait_ge(x_new, updated + k + 1)
                    nc.scalar.mul(operand[:, k, 0:T], xs[:, k, :], param[:, gain + k:gain + k + 1]).then_inc(op_hi, 1)
                for c in range(4):
                    nc.scalar.activation(squares[:, 4 * c:4 * c + 4, :], xs[:, 4 * c:4 * c + 4, :],
                                         ACT.Square).then_inc(x_squared, 1)

            def ffn(up_base, down_base, g_up, g_down, m, n_op, gain, updated, n_h, n_sq):
                operand_hi(n_op, gain, updated)
                for n, s in tiles(act, KF, 4, 2):
                    a = up_base + 4 * s
                    for j in range(4):
                        if not (s == 0 and up_base):
                            split_hi(n * 4 + (up_base + j), a + j)
                        if s >= 2 and j == 0:
                            silu(n - 2, s - 2, n_h)
                        if s >= 2 and j == 1:
                            hidden_hi(n - 2, n_h)
                    if s == 1:
                        root(m, pre_scale[:, :], 1.0 / D, 0)
                    if s >= 1:
                        right(n * 4 + up_base, n + (g_up - 1), 2 * ((s - 1) % 2), 2, t2)
                for j in range(4):
                    split_hi(down_base + j, down_base + j)
                    if j == 0:
                        silu(KF - 2, KF - 2, n_h)
                    if j == 1:
                        hidden_hi(KF - 2, n_h)
                right(down_base, g_up + KF - 1, 2 * ((KF - 1) % 2), 2, t2)
                silu(KF - 1, KF - 1, n_h)
                hidden_hi(KF - 1, n_h)
                for d, s in tiles(act, KD, 4, 4):
                    for j in range(DOWN_PIECES):
                        if not (s == 0 and j < 4):
                            split_hi(d * DOWN_PIECES + (down_base + j), down_base + s * DOWN_PIECES + j)
                        if s >= 1 and j == 3:
                            right(d * DOWN_PIECES + down_base, d + (g_down - 1), (s + 1) % 4, 1, t2[:, 0:1, :])
                        if s >= 1 and j == 4:
                            square_f(d - 1, s - 1, d + (g_down - 1), n_sq)

            def after_down(down_base, g_down, n_sq, m, scale, eps_col, last=False):
                nxt = down_base
                if not last:
                    for j in range(3):
                        split_hi(nxt + j, nxt + j)
                right(REC if g_down == G_DOWN1 else END, g_down + KD - 1, (KD + 1) % 4, 1, t2[:, 0:1, :])
                square_f(KD - 1, KD - 1, g_down + KD - 1, n_sq)
                if not last:
                    split_hi(nxt + 3, nxt + 3)
                root(m, post_scale[:, :], scale, eps_col)

            act.wait_ge(params_loaded, 16)
            lam = param[:, C_LAM:C_LAM + REC_TILES]
            ffn(UP1, DOWN1, G_UP1, G_DOWN1, 0, 0, C_FFN1_PRE, None, 0, 0)
            after_down(REC, G_DOWN1, 0, 1, 4.0 / D, 1)

            operand_hi(KD, C_MIX_PRE, 0)
            nc.scalar.activation(soft[:, 0, :], lam, ACT.Abs).then_inc(soft_act, 1)
            act.wait_ge(soft_act, 1)
            nc.scalar.activation(soft[:, 1, :], soft[:, 0, :], ACT.Exp, scale=-1.0).then_inc(soft_act, 1)

            def conv_first(n, s):
                act.wait_ge(scaled, n + (KF + 1))
                if s >= 2:
                    act.wait_ge(gates_done, n - 1)
                    act.wait_ge(rec_step, n * 5 - 5)
                col = lambda c: param[:, bass.ds(n + c, 1)]
                nc.scalar.activation(conv[:, s % 2, :], xg[:, 0, 1:T + 1], ACT.Identity,
                                     bias=col(C_CONV_B), scale=col(C_CONV_W)).then_inc(conv0, 1)

            def gr_square(n, s):
                if s >= 1:
                    act.wait_ge(gelu_done, n)
                nc.scalar.activation(gelu_tmp[:, :], xg[:, 1, 4:T + 4], ACT.Square).then_inc(gr_squared, 1)

            def gelu_tanh(n):
                act.wait_ge(gelu_step, n * 2 + 2)
                nc.scalar.activation(gelu_tmp[:, :], gelu_tmp[:, :], ACT.Tanh, scale=GELU_S).then_inc(gelu_th, 1)

            def gate_tanhs(n, s):
                act.wait_ge(gates_done, n + 1)
                if s == 0:
                    act.wait_ge(soft_step, 15)
                if s >= 1:
                    act.wait_ge(rec_step, n * 5)
                const = lambda c: rec_const[:, c, bass.ds(n, 1)]
                nc.scalar.activation(gate_t[:, 0, :], banks[:, 6, 0:T], ACT.Tanh, bias=const(0), scale=0.5)\
                    .then_inc(gate_tanh, 1)
                nc.scalar.activation(gate_t[:, 1, :], banks[:, 6, T:2 * T], ACT.Tanh, bias=const(1), scale=0.5)\
                    .then_inc(gate_tanh, 1)
                act.wait_ge(gate_tanh, n * 3 + 2)
                nc.scalar.activation(tanh_la[:, bass.ds(n, 1), :].rearrange("p a t -> p (a t)"), gate_t[:, 0, :],
                                     ACT.Tanh, bias=const(2), scale=const(2)).then_inc(gate_tanh, 1)

            def rec_stages(n, s, j):
                if j == 0 and 2 <= s < REC_TILES + 2:
                    conv_first(n - 2, s - 2)
                    gr_square(n - 2, s - 2)
                if j == 1 and 2 <= s < REC_TILES + 2:
                    gelu_tanh(n - 2)
                if j == 2 and 3 <= s < REC_TILES + 3:
                    gate_tanhs(n - 3, s - 3)

            for n, s in tiles(act, REC_TILES, 4, 2):
                for j in range(4):
                    if s >= 1:
                        split_hi(n * 4 + (REC + j), REC + 4 * s + j)
                    rec_stages(n, s, j)
                if s == 1:
                    root(2, pre_scale[:, :], 1.0 / D, 0)
                if s >= 1:
                    right(n * 4 + REC, n + (G_REC - 1), 2 * (s % 2), 2, t2)

            def softmax_exp(h):
                act.wait_ge(softmax_step, 4 * h + 4)
                scale = P ** -0.5
                nc.scalar.activation(prob[:, 0:P], prob[:, 0:P], ACT.Exp, bias=stat[:, 2:3], scale=scale,
                                     accum_out=stat[:, 4:5]).then_inc(exp_done, 1)
                nc.scalar.activation(prob[:, P:3 * P], prob[:, P:3 * P], ACT.Exp, bias=stat[:, 3:4], scale=scale,
                                     accum_out=stat[:, 5:6]).then_inc(exp_done, 1)

            def copy_v(h):
                act.wait_ge(v_turned, h + 1)
                if h >= 1:
                    act.wait_ge(pv_done, h)
                nc.scalar.copy(v_rows[:, :, :].rearrange("p a t -> p (a t)"), banks[:, 7, 0:T]).then_inc(v_copied, 1)

            def copy_probs(h):
                act.wait_ge(p_turned, h + 1)
                nc.scalar.copy(prob_t, banks[:, 6, 0:3 * P]).then_inc(p_copied, 1)

            def copy_att(h):
                act.wait_ge(pv_done, h + 1)
                nc.scalar.copy(att[:, h, :], banks[:, 7, T:2 * T]).then_inc(att_copied, 1)
                act.wait_ge(att_copied, h + 1)
                if h >= 1:
                    act.wait_ge(att_sum, h)
                else:
                    act.wait_ge(gelu_done, REC_TILES)
                nc.scalar.activation(squares_att, att[:, h, :], ACT.Square).then_inc(att_sqd, 1)

            squares_att = gelu_tmp[:, :]

            def root_tanh():
                act.wait_ge(gate_tanh, 3 * REC_TILES)
                nc.scalar.activation(tanh_la[:, :, :], tanh_la[:, :, :], ACT.Sqrt).then_inc(root_t, 1)

            def rec_square(j):
                act.wait_ge(rec_done, j + 1)
                if j >= 1:
                    act.wait_ge(rec_sum, j)
                nc.scalar.activation(rec_sq[:, :], gated_in[:, j, :], ACT.Square).then_inc(rec_sqd, 1)

            for h in range(HEADS + 1):
                base = ATT + 6 * h
                for j in range(6 if h < HEADS else 4):
                    split_hi(base + j, base + j)
                    if h < 2 and j < 2 or h == 0 and j == 2:
                        rec_stages(REC_TILES + h, REC_TILES + h, j)
                    if h < 2 and j == 5:
                        gate_tanhs(REC_TILES - 2 + h, REC_TILES - 2 + h)
                    if h >= 2 and j == 0:
                        copy_v(h - 2)
                    if h >= 2 and j == 1:
                        softmax_exp(h - 2)
                    if j == 3 and h == 0:
                        right(ATT, G_ATT - 1, 2 * (REC_TILES % 2), 2, t2)
                    if j == 3 and h >= 1:
                        right(base, G_ATT + h - 1, 3 * (h % 2), 3, t3)
                    if j == 3 and h >= 2:
                        copy_probs(h - 2)
                    if h == 3 and j == 0:
                        root_tanh()
                    if 3 <= h <= 6 and j in (3, 5):
                        rec_square(2 * (h - 3) + (j == 5))
                if h >= 2 and h < HEADS:
                    copy_att(h - 2)

            def merged_hi(k):
                act.wait_ge(m_f, k + 1)
                nc.scalar.copy(merged[:, k, 0:T], (gated_in if k < PIECE else att)[:, k % PIECE, :]).then_inc(m_hi, 1)

            root(3, post_scale[:, :], 1.0 / (REC_TILES * P), 0)
            copy_att(HEADS - 2)
            copy_v(HEADS - 1)
            for k in range(PIECE):
                merged_hi(k)
            softmax_exp(HEADS - 1)
            copy_probs(HEADS - 1)
            for n in range(OUT + 4, OUT + 6):
                split_hi(n, n)
            copy_att(HEADS - 1)
            for n in range(OUT + 6, OUT + 8):
                split_hi(n, n)
            root(4, pre_scale[:, :], 1.0 / (HEADS * P), 0)
            for k in range(PIECE, KD):
                merged_hi(k)

            for g, s in tiles(act, KD // 4 - 1, 1, 1):
                for j in range(8):
                    split_hi(g * 8 + (OUT + 8 + j), OUT + 8 + s * 8 + j)
                    if j < 4:
                        right(g * 8 + (OUT + 5 + j), g * 4 + (G_OUT + j), j, 1, t2[:, 0:1, :])
                        square_f(g * 4 + j, s * 4 + j, g * 4 + (G_OUT + j), KD)
            for j in range(4):
                split_hi(UP2 + j, UP2 + j)
                e = G_OUT + KD - 4 + j
                right(UP2 - 3 + j, e, j, 1, t2[:, 0:1, :])
                square_f(KD - 4 + j, KD - 4 + j, e, KD)
            root(5, post_scale[:, :], 1.0 / D, 0)
            ffn(UP2, DOWN2, G_UP2, G_DOWN2, 6, 2 * KD, C_FFN2_PRE, KD, KF, 2 * KD)
            after_down(0, G_DOWN2, 2 * KD, 7, 4.0 / D, 1, last=True)

        @block.vector
        def _(dve):
            v = nc.vector

            def split_lo(n, s):
                dve.wait_ge(hi_done, n + 1)
                cols = slice(0, size_of(s))
                v.tensor_tensor(w_lo[:, s % SLOTS, cols], raw[:, s % SLOTS, cols],
                                w_hi[:, s % SLOTS, cols].bitcast(F32), ALU.subtract).then_inc(lo_done, 1)

            def add_halves(e, bank, n, src, dst):
                dve.wait_ge(right_half, e + 1)
                v.tensor_tensor(dst, banks[:, bank:bank + n, 0:T], src, ALU.add).then_inc(evacuated, 1)

            def scale_tokens(e, ap, n, count):
                dve.wait_ge(evacuated, e + 1)
                v.tensor_tensor(ap, ap, both(pre_scale[:, :], n), ALU.mult).then_inc(scaled, 1)

            def gate_hidden(n, n_h):
                dve.wait_ge(silu_done, n + (n_h + 1))
                v.tensor_tensor(sg, sg, gu[:, 1, :], ALU.mult).then_inc(gated, 1)

            def hidden_lo(n, n_h):
                dve.wait_ge(h_hi, n + (n_h + 1))
                col = bass.ds(n, 1)
                v.tensor_tensor(hidden[:, col, T:2 * T].rearrange("p a t -> p (a t)"), sg,
                                hidden[:, col, 0:T].rearrange("p a t -> p (a t)").bitcast(F32), ALU.subtract)\
                    .then_inc(h_lo, 1)

            def inverse(m, ap):
                dve.wait_ge(norm_root, m + 1)
                v.reciprocal(ap, ap).then_inc(norm_ready, 1)

            def add_square(d, s, n_sq):
                dve.wait_ge(sq_done, d + (n_sq + 1))
                if s == 0:
                    v.tensor_copy(post_scale[:, :], sq).then_inc(sq_summed, 1)
                else:
                    dve.wait_ge(sq_summed, d + n_sq)
                    v.tensor_tensor(post_scale[:, :], post_scale[:, :], sq, ALU.add).then_inc(sq_summed, 1)

            def tree_sum(count):
                dve.wait_ge(x_squared, 4 * (count + 1))
                for level, half in enumerate((8, 4, 2, 1)):
                    if level:
                        dve.wait_ge(tree, 4 * count + level)
                    v.tensor_tensor(squares[:, 0:half, :], squares[:, 0:half, :], squares[:, half:2 * half, :],
                                    ALU.add).then_inc(tree, 1)

            def update_x(m, n_f, post_gain, pre_gain, n_op):
                dve.wait_ge(norm_ready, m + 1)
                for k in range(KD + 1):
                    if k < KD:
                        v.scalar_tensor_tensor(f[:, k, :], f[:, k, :], param[:, post_gain + k:post_gain + k + 1],
                                               post_scale[:, :], ALU.mult, ALU.mult).then_inc(f_scaled, 1)
                    if k and pre_gain is not None:
                        operand_lo(k - 1, pre_gain, n_op)

            def operand_lo(k, pre_gain, n_op):
                dve.wait_ge(op_hi, n_op + k + 1)
                v.scalar_tensor_tensor(operand[:, k, T:2 * T], xs[:, k, :], param[:, pre_gain + k:pre_gain + k + 1],
                                       operand[:, k, 0:T].bitcast(F32), ALU.mult, ALU.subtract).then_inc(op_lo, 1)

            def ffn(up_base, down_base, g_up, g_down, m, n_h, n_sq, count):
                tree_sum(count)
                for n, s in tiles(dve, KF, 4, 2):
                    a = up_base + 4 * s
                    for j in range(4):
                        if s >= 2 and j == 0:
                            add_halves(n + (g_up - 2), 2 * (s % 2), 2, t2, gu)
                            scale_tokens(n + (g_up - 2), gu, 2, None)
                        if not (s == 0 and up_base):
                            split_lo(n * 4 + (up_base + j), a + j)
                        if s >= 2 and j == 0:
                            gate_hidden(n - 2, n_h)
                        if s >= 2 and j == 1:
                            hidden_lo(n - 2, n_h)
                    if s == 1:
                        inverse(m, pre_scale[:, :])
                        dve.wait_ge(norm_ready, m + 1)
                for j in range(4):
                    if j == 0:
                        add_halves(g_up + KF - 2, 2 * ((KF - 2) % 2), 2, t2, gu)
                        scale_tokens(g_up + KF - 2, gu, 2, None)
                    split_lo(down_base + j, down_base + j)
                    if j == 0:
                        gate_hidden(KF - 2, n_h)
                    if j == 1:
                        hidden_lo(KF - 2, n_h)
                add_halves(g_up + KF - 1, 2 * ((KF - 1) % 2), 2, t2, gu)
                scale_tokens(g_up + KF - 1, gu, 2, None)
                gate_hidden(KF - 1, n_h)
                hidden_lo(KF - 1, n_h)
                for d, s in tiles(dve, KD, 4, 4):
                    for j in range(DOWN_PIECES):
                        if not (s == 0 and j < 4):
                            split_lo(d * DOWN_PIECES + (down_base + j), down_base + s * DOWN_PIECES + j)
                        if s >= 1 and j == 3:
                            add_halves(d + (g_down - 1), (s + 1) % 4, 1, t2[:, 0:1, :], f[:, bass.ds(d - 1, 1), :])
                        if s >= 1 and j == 4:
                            add_square(d - 1, s - 1, n_sq)

            def after_down(nxt, g_down, n_sq, m, last=False):
                if not last:
                    for j in range(3):
                        split_lo(nxt + j, nxt + j)
                add_halves(g_down + KD - 1, (KD + 1) % 4, 1, t2[:, 0:1, :], f[:, KD - 1:KD, :])
                add_square(KD - 1, KD - 1, n_sq)
                if not last:
                    split_lo(nxt + 3, nxt + 3)
                inverse(m, post_scale[:, :])

            v.memset(ones[:, :], 1.0).then_inc(ones_set, 1)
            dve.wait_ge(params_loaded, 16)
            for k in range(KD):
                if k % 4 == 0:
                    dve.wait_ge(x_loaded[k // 4], 16)
                operand_lo(k, C_FFN1_PRE, 0)
            ffn(UP1, DOWN1, G_UP1, G_DOWN1, 0, 0, 0, 0)
            after_down(REC, G_DOWN1, 0, 1)
            update_x(1, 0, C_FFN1_POST, C_MIX_PRE, KD)
            dve.wait_ge(f_scaled, KD)
            dve.wait_ge(x_new, KD)
            v.memset(gate_w[:, :, :, :], 0.0).then_inc(pads_zero, 1)
            v.memset(xg[:, :, 0:4], 0.0).then_inc(pads_zero, 1)
            tree_sum(1)

            lam = param[:, C_LAM:C_LAM + REC_TILES]
            z, z2, series = soft[:, 3, :], soft[:, 4, :], soft[:, 5, :]
            steps = [0]

            def chained(ins):
                ins.then_inc(soft_step, 1)
                steps[0] += 1
                dve.wait_ge(soft_step, steps[0])

            dve.wait_ge(soft_act, 2)
            e = soft[:, 1, :]
            chained(v.tensor_scalar(soft[:, 2, :], e, 2.0, None, ALU.add))
            chained(v.reciprocal(soft[:, 6, :], soft[:, 2, :]))
            chained(v.tensor_tensor(z, e, soft[:, 6, :], ALU.mult))
            chained(v.tensor_tensor(z2, z, z, ALU.mult))
            chained(v.tensor_scalar(series, z2, 1.0 / 15, None, ALU.mult))
            for odd in (13, 11, 9, 7, 5, 3):
                chained(v.scalar_tensor_tensor(series, series, 1.0 / odd, z2, ALU.add, ALU.mult))
            chained(v.scalar_tensor_tensor(series, series, 1.0, z, ALU.add, ALU.mult))
            chained(v.tensor_scalar(rec_const[:, 0:2, :].rearrange("p a t -> p (a t)"),
                                    param[:, C_BA:C_BX + REC_TILES], 0.5, None, ALU.mult))
            chained(v.tensor_scalar(soft[:, 7, :], lam, -2.0, 0.0, ALU.mult, ALU.max))
            chained(v.scalar_tensor_tensor(rec_const[:, 2, :], series, 4.0, soft[:, 7, :], ALU.mult, ALU.add))

            def conv_rest(n, s):
                dve.wait_ge(conv0, n + 1)
                for tap in (1, 2, 3):
                    if tap > 1:
                        dve.wait_ge(conv_step, n * 2 + (tap - 1))
                    ins = v.scalar_tensor_tensor(conv[:, s % 2, :], xg[:, 0, 1 + tap:T + 1 + tap],
                                                 param[:, bass.ds(n + (C_CONV_W + REC_TILES * tap), 1)],
                                                 conv[:, s % 2, :], ALU.mult, ALU.add)
                    ins.then_inc(conv_step if tap < 3 else conv_done, 1)

            def recurrence_inputs(n, s):
                tile = lambda a: a[:, bass.ds(n, 1), :].rearrange("p a t -> p (a t)")
                dve.wait_ge(gate_tanh, n * 3 + 3)
                v.tensor_scalar(q_rec[:, :], tile(tanh_la), 1.0, None, ALU.add).then_inc(rec_step, 1)
                v.scalar_tensor_tensor(tile(gated_in), gate_t[:, 1, :], 1.0, conv[:, s % 2, :], ALU.add, ALU.mult)\
                    .then_inc(rec_step, 1)
                dve.wait_ge(rec_step, n * 5 + 1)
                v.reciprocal(q_rec[:, :], q_rec[:, :]).then_inc(rec_step, 1)
                dve.wait_ge(rec_step, n * 5 + 3)
                v.tensor_scalar(tile(decay), q_rec[:, :], 2.0, -1.0, ALU.mult, ALU.add).then_inc(rec_step, 1)
                v.tensor_tensor(tile(gated_in), tile(gated_in), q_rec[:, :], ALU.mult).then_inc(rec_step, 1)

            def rec_stages(n, s, j):
                if j == 0 and 2 <= s < REC_TILES + 2:
                    conv_rest(n - 2, s - 2)
                if j == 3 and 3 <= s < REC_TILES + 3:
                    recurrence_inputs(n - 3, s - 3)

            def rec_evacuate(n, s):
                e_ = n + G_REC
                if s >= 1:
                    dve.wait_ge(gelu_done, n)
                    dve.wait_ge(conv_done, n)
                add_halves(e_, 2 * ((s + 1) % 2), 2, t2, xg[:, :, 4:T + 4])
                scale_tokens(e_, xg[:, :, 4:T + 4], 2, None)

            for n, s in tiles(dve, REC_TILES, 4, 2):
                for j in range(4):
                    if j == 0 and s >= 2:
                        rec_evacuate(n - 2, s - 2)
                    if s >= 1:
                        split_lo(n * 4 + (REC + j), REC + 4 * s + j)
                    rec_stages(n, s, j)
                if s == 1:
                    inverse(2, pre_scale[:, :])
                    dve.wait_ge(norm_ready, 3)

            def rotate(h):
                qk = qkv[0:32, 0:2, :]
                dve.wait_ge(scaled, KF + REC_TILES + h + 1)
                v.stream_shuffle(rope_tmp[:, :, :], qk, list(range(16, 32)) + list(range(16))).then_inc(rope_step, 1)
                dve.wait_ge(rope_step, 4 * h + 1)
                v.tensor_tensor(rope_tmp[:, :, :], rope_tmp[:, :, :], rope_t[:, 1:2, :].to_broadcast([32, 2, T]),
                                ALU.mult).then_inc(rope_step, 1)
                v.tensor_tensor(qk, qk, rope_t[:, 0:1, :].to_broadcast([32, 2, T]), ALU.mult).then_inc(rope_step, 1)
                dve.wait_ge(rope_step, 4 * h + 3)
                v.tensor_tensor(qk, qk, rope_tmp[:, :, :], ALU.add).then_inc(rope_step, 1)

            def softmax_max(h):
                dve.wait_ge(scored, h + 1)
                if h >= 1:
                    dve.wait_ge(p_turned, h)
                v.tensor_tensor(prob, banks[:, 6, 0:3 * P], mask[:, :], ALU.add).then_inc(softmax_step, 1)
                dve.wait_ge(softmax_step, 4 * h + 1)
                v.tensor_reduce(stat[:, 0:1], prob[:, 0:P], AX.X, ALU.max).then_inc(softmax_step, 1)
                v.tensor_reduce(stat[:, 1:2], prob[:, P:3 * P], AX.X, ALU.max).then_inc(softmax_step, 1)
                dve.wait_ge(softmax_step, 4 * h + 3)
                v.tensor_scalar(stat[:, 2:4], stat[:, 0:2], -(P ** -0.5), None, ALU.mult).then_inc(softmax_step, 1)

            def softmax_divide(h):
                dve.wait_ge(exp_done, 2 * h + 2)
                v.reciprocal(stat[:, 6:8], stat[:, 4:6]).then_inc(rec_den, 1)
                dve.wait_ge(rec_den, h + 1)
                v.tensor_scalar(prob[:, 0:P], prob[:, 0:P], stat[:, 6:7], None, ALU.mult).then_inc(p_ready, 1)
                v.tensor_scalar(prob[:, P:3 * P], prob[:, P:3 * P], stat[:, 7:8], None, ALU.mult).then_inc(p_ready, 1)

            def scan(j):
                dve.wait_ge(u_done, j + 1)
                v.tensor_tensor_scan(decay[:, j, :], decay[:, j, :], gated_in[:, j, :], 0.0, ALU.mult, ALU.add)\
                    .then_inc(scan_step, 1)
                dve.wait_ge(scan_step, j + 1)
                dve.wait_ge(gelu_done, REC_TILES)
                v.scalar_tensor_tensor(gated_in[:, j, :], decay[:, j, :], 0.5, gelu[:, j, :], ALU.mult, ALU.mult)\
                    .then_inc(rec_done, 1)

            def att_evacuate(h):
                if h >= 1:
                    dve.wait_ge(v_turned, h)
                    dve.wait_ge(scored, h)
                add_halves(G_ATT + h, 3 * ((h + 1) % 2), 3, t3, qkv[:, :, :])
                scale_tokens(G_ATT + h, qkv[:, :, :], 3, None)
                rotate(h)

            dve.wait_ge(mixer_loaded, 7 * 16)
            for h in range(HEADS + 1):
                base = ATT + 6 * h
                for j in range(6 if h < HEADS else 4):
                    if h < 2 and j == 0:
                        rec_evacuate(REC_TILES - 2 + h, REC_TILES - 2 + h)
                    split_lo(base + j, base + j)
                    if h < 2 and j == 0 or h == 0 and j == 3:
                        rec_stages(REC_TILES + h, REC_TILES + h, j)
                    if h < 2 and j == 5:
                        recurrence_inputs(REC_TILES - 2 + h, REC_TILES - 2 + h)
                    if h >= 2 and j == 0:
                        softmax_max(h - 2)
                    if h >= 2 and j == 2:
                        softmax_divide(h - 2)
                    if h >= 1 and j == 3:
                        att_evacuate(h - 1)
                    if 3 <= h <= 6 and j in (2, 4):
                        scan(2 * (h - 3) + (j == 4))

            def merge(k, m):
                src = (gated_in if k < PIECE else att)[:, k % PIECE, :]
                norm = post_scale if k < PIECE else pre_scale
                v.scalar_tensor_tensor(src, src, param[:, C_REC_OUT + k:C_REC_OUT + k + 1], norm[:, :],
                                       ALU.mult, ALU.mult).then_inc(m_f, 1)

            def merged_lo(k):
                dve.wait_ge(m_hi, k + 1)
                src = (gated_in if k < PIECE else att)[:, k % PIECE, :]
                v.tensor_tensor(merged[:, k, T:2 * T], src, merged[:, k, 0:T].bitcast(F32), ALU.subtract)\
                    .then_inc(m_lo, 1)

            inverse(3, post_scale[:, :])
            dve.wait_ge(norm_ready, 4)
            softmax_max(HEADS - 1)
            for k in range(PIECE):
                merge(k, 3)
            for k in range(PIECE):
                merged_lo(k)
            softmax_divide(HEADS - 1)
            for n in range(OUT + 4, OUT + 8):
                split_lo(n, n)
            inverse(4, pre_scale[:, :])
            dve.wait_ge(norm_ready, 5)
            for k in range(PIECE, KD + 1):
                if k < KD:
                    merge(k, 4)
                if k > PIECE:
                    merged_lo(k - 1)

            for g, s in tiles(dve, KD // 4 - 1, 1, 1):
                for j in range(8):
                    split_lo(g * 8 + (OUT + 8 + j), OUT + 8 + s * 8 + j)
                    if j < 4:
                        add_halves(g * 4 + (G_OUT + j), j, 1, t2[:, 0:1, :], f[:, bass.ds(g * 4 + j, 1), :])
                        add_square(g * 4 + j, s * 4 + j, KD)
            for j in range(4):
                split_lo(UP2 + j, UP2 + j)
                k = KD - 4 + j
                add_halves(G_OUT + k, j, 1, t2[:, 0:1, :], f[:, k:k + 1, :])
                add_square(k, k, KD)
            inverse(5, post_scale[:, :])
            update_x(5, KD, C_MIX_POST, C_FFN2_PRE, 2 * KD)
            ffn(UP2, DOWN2, G_UP2, G_DOWN2, 6, KF, 2 * KD, 2)
            after_down(0, G_DOWN2, 2 * KD, 7, last=True)
            update_x(7, 2 * KD, C_FFN2_POST, None, None)

        @block.gpsimd
        def _(pool):
            p = nc.gpsimd

            def add_f(n):
                for k in range(KD):
                    pool.wait_ge(f_scaled, n * KD + k + 1)
                    p.tensor_tensor(xs[:, k, :], xs[:, k, :], f[:, k, :], ALU.add).then_inc(x_new, 1)

            add_f(0)
            pool.wait_ge(mixer_loaded, 7 * 16)
            for n in range(REC_TILES):
                if n >= 2:
                    pool.wait_ge(gates_done, n - 1)
                p.tensor_copy(gate_w2[:, n % 2, :, :], gate_w[:, n, :, :]).then_inc(gatew_now, 1)
                pool.wait_ge(gr_squared, n + 1)
                pool.wait_ge(scaled, KF + n + 1)
                gr = xg[:, 1, 4:T + 4]
                p.tensor_scalar(gelu_tmp[:, :], gelu_tmp[:, :], GELU_C, 1.0, ALU.mult, ALU.add).then_inc(gelu_step, 1)
                pool.wait_ge(gelu_step, 2 * n + 1)
                p.tensor_tensor(gelu_tmp[:, :], gelu_tmp[:, :], gr, ALU.mult).then_inc(gelu_step, 1)
                pool.wait_ge(gelu_th, n + 1)
                p.tensor_tensor(gelu[:, n, :], gelu_tmp[:, :], gr, ALU.mult).then_inc(gelu_mul, 1)
                pool.wait_ge(gelu_mul, n + 1)
                p.tensor_tensor(gelu[:, n, :], gelu[:, n, :], gr, ALU.add).then_inc(gelu_done, 1)
            pool.wait_ge(root_t, 1)
            pool.wait_ge(rec_step, 5 * REC_TILES)

            def u(j):
                p.tensor_tensor(gated_in[:, j, :], gated_in[:, j, :], tanh_la[:, j, :], ALU.mult).then_inc(u_done, 1)

            def add_rec_square(j):
                pool.wait_ge(rec_sqd, j + 1)
                if j == 0:
                    p.tensor_copy(post_scale[:, :], rec_sq[:, :]).then_inc(rec_sum, 1)
                else:
                    pool.wait_ge(rec_sum, j)
                    p.tensor_tensor(post_scale[:, :], post_scale[:, :], rec_sq[:, :], ALU.add).then_inc(rec_sum, 1)

            def add_att_square(h):
                pool.wait_ge(att_sqd, h + 1)
                if h == 0:
                    p.tensor_copy(att_total[:, :], gelu_tmp[:, :]).then_inc(att_sum, 1)
                elif h < HEADS - 1:
                    pool.wait_ge(att_sum, h)
                    p.tensor_tensor(att_total[:, :], att_total[:, :], gelu_tmp[:, :], ALU.add).then_inc(att_sum, 1)
                else:
                    pool.wait_ge(att_sum, h)
                    pool.wait_ge(scaled, KF + REC_TILES + HEADS)
                    p.tensor_tensor(pre_scale[:, :], att_total[:, :], gelu_tmp[:, :], ALU.add).then_inc(att_sum, 1)

            for j in range(2):
                u(j)
            add_att_square(0)
            for h in range(3, 7):
                for j in (2 * (h - 3), 2 * (h - 3) + 1):
                    if j + 2 < REC_TILES:
                        u(j + 2)
                    add_rec_square(j)
                add_att_square(h - 2)
            for h in range(5, HEADS):
                add_att_square(h)
            add_f(1)
            add_f(2)


def weight_tiles(w, order):
    k, n = w.shape
    tiled = w.reshape(k // P, P, n // P, P).transpose(2, 1, 0, 3)
    return np.ascontiguousarray(tiled[order]).reshape(n // P, P, k)


def channels(vector):
    return vector.reshape(-1, P).T


def kernel(x, ffn1_pre_g, ffn1_w_gate_up, ffn1_w_down, ffn1_post_g, mix_pre_g, w_in, conv_w, conv_b,
           rg_w_a, rg_b_a, rg_w_x, rg_b_x, rg_lambda, attn_out_g, rec_out_g, w_out, mix_post_g,
           ffn2_pre_g, ffn2_w_gate_up, ffn2_w_down, ffn2_post_g):
    import concourse.bacc as bacc
    from concourse.bass_utils import run_bass_kernel_spmd

    n = lambda a: np.asarray(a)
    pairs = [i for t in range(KF) for i in (t, KF + t)]
    rec_order = [i for t in range(8) for i in (24 + t, 32 + t)]
    att_order = [i for t in range(8) for i in (t, 8 + t, 16 + t)]
    w_in = n(w_in)[0]
    in_tiles = weight_tiles(w_in, list(range(40)))
    w_out_rec_first = np.concatenate([n(w_out)[0][D // 2:], n(w_out)[0][:D // 2]])
    plain = list(range(KD))

    eps = np.full((P, 2), EPS, np.float32)
    eps[:, 1] = 4 * EPS
    columns = [channels(n(a)[0]) for a in (
        ffn1_pre_g, ffn1_post_g, mix_pre_g, rec_out_g, attn_out_g, mix_post_g, ffn2_pre_g, ffn2_post_g,
        conv_w, conv_b, rg_b_a, rg_b_x, rg_lambda)] + [eps]
    gates = np.stack([n(g)[0].reshape(8, 2, 64, 64).transpose(1, 2, 0, 3) for g in (rg_w_a, rg_w_x)])

    rot = 32
    inv_freq = np.float32(500000.0) ** (-np.arange(0, rot, 2, dtype=np.float32) / np.float32(rot))
    angle = (np.arange(T, dtype=np.float32)[:, None] * inv_freq.astype(np.float32)[None, :]).T
    cos, sin = np.cos(angle).astype(np.float32), np.sin(angle).astype(np.float32)
    rope = np.stack([np.concatenate([cos, cos]), np.concatenate([-sin, sin])], axis=1)
    causal = np.where(np.arange(P)[None, :] <= np.arange(P)[:, None], 0.0, MASKED).astype(np.float32)
    consts = np.concatenate([causal, causal, np.zeros((P, P), np.float32), np.eye(P, dtype=np.float32)], axis=1)

    ins = {
        "x_in": n(x)[0].reshape(T, KD, P).transpose(2, 1, 0),
        "up1_w": weight_tiles(n(ffn1_w_gate_up)[0], pairs),
        "down1_w": weight_tiles(n(ffn1_w_down)[0], plain),
        "rec_w": in_tiles[rec_order],
        "att_w": in_tiles[att_order],
        "out_w": weight_tiles(w_out_rec_first, plain),
        "up2_w": weight_tiles(n(ffn2_w_gate_up)[0], pairs),
        "down2_w": weight_tiles(n(ffn2_w_down)[0], plain),
        "params": np.concatenate(columns, axis=1),
        "gates": gates,
        "rope": rope,
        "consts": consts,
    }
    ins = {name: np.ascontiguousarray(a) for name, a in ins.items()}
    nc = bacc.Bacc("TRN2", target_bir_lowering=False, num_devices=1)
    args = [nc.dram_tensor(name, a.shape, F32, kind="ExternalInput").ap() for name, a in ins.items()]
    y = nc.dram_tensor("y_out", (P, KD, T), F32, kind="ExternalOutput").ap()
    layer(nc, *args, y)
    got = run_bass_kernel_spmd(nc, [ins], core_ids=[0]).results[0]["y_out"]
    return np.ascontiguousarray(got.transpose(2, 1, 0)).reshape(1, T, D)
```

```python
from contextlib import ExitStack

import numpy as np

import concourse.bass as bass
from concourse import mybir
from concourse.alu_op_type import AluOpType as ALU

ACT = mybir.ActivationFunctionType
AX = mybir.AxisListType
F32 = mybir.dt.float32
F32R = mybir.dt.float32r

P = 128
T = 256
D = 2048
KD = D // P
FF = ((8 * D // 3 + 127) // 128) * 128
KF = FF // P
HEADS = 8
REC_TILES = 8
PIECE = 8
DOWN_PIECES = -(-KF // PIECE)
SLOTS = 4
EPS = 1e-6
MASKED = -3.0e38
OUT_BANKS = (3, 4, 0, 1)
GELU_C = 0.044715
GELU_S = float(np.sqrt(2.0 / np.pi))

UP1, DOWN1, REC, ATT = 0, 4 * KF, 4 * KF + DOWN_PIECES * KD, 4 * KF + DOWN_PIECES * KD + 4 * REC_TILES
OUT = ATT + 6 * HEADS
UP2 = OUT + 2 * KD
DOWN2 = UP2 + 4 * KF
END = DOWN2 + DOWN_PIECES * KD
G_UP1, G_DOWN1 = 0, KF
G_REC = G_DOWN1 + KD
G_ATT = G_REC + REC_TILES
G_OUT = G_ATT + HEADS
G_UP2 = G_OUT + 2 * KD
G_DOWN2 = G_UP2 + KF
assert all(n % SLOTS == 0 for n in (DOWN1, REC, ATT, OUT, UP2, DOWN2, END))

N_SQ = (0, KD - 1, 2 * KD - 3)

UPDATE_HI, UPDATE_LO = 11, {10: 3, 14: 4}

GAINED = (0, KD - 1, 2 * KD - 1, 3 * KD - 2)

C_FFN1_PRE, C_FFN1_POST, C_MIX_PRE, C_REC_OUT, C_ATT_OUT, C_MIX_POST, C_FFN2_PRE, C_FFN2_POST = (
    0, 16, 32, 48, 56, 64, 80, 96)
C_CONV_W, C_CONV_B, C_BA, C_BX, C_LAM, C_EPS = 112, 144, 152, 160, 168, 176
N_PARAM = 178


def tiles(eng, count, peel, unroll, tail=0):
    for n in range(peel):
        yield n, n
    rounds = (count - peel - tail) // unroll
    if rounds:
        with eng.Fori(0, rounds) as i:
            for r in range(unroll):
                yield i * unroll + (peel + r), peel + r
    for n in range(peel + rounds * unroll, count):
        yield n, n


def layer(nc, x, up1, down1, rec_in, att_in, out_w, up2, down2, params, gates, rope, consts, y):
    with ExitStack() as ctx:
        def sem(name):
            return ctx.enter_context(nc.semaphore(name))

        top = [(nc.sbuf_base + 63) // 64 * 64]

        def place(name, shape, dtype=F32, at=None):
            size = -(-4 * int(np.prod(shape[1:])) // 32) * 32
            offset = top[0] if at is None else at[0]
            if at is None:
                top[0] += size
            else:
                at[0] += size
            return nc.alloc_sbuf_tensor_at(name, shape, dtype, offset=offset)

        raw = place("weights_raw", [P, SLOTS, PIECE * P])
        w_hi = place("weights_hi", [P, SLOTS, PIECE * P], F32R)
        w_lo = place("weights_lo", [P, SLOTS, PIECE * P], F32R)
        xs = place("x_residual", [P, KD, T])
        operand = place("operand_hi_lo", [P, KD, 2 * T], F32R)
        param = place("channel_params", [P, N_PARAM])
        ones = place("ones", [P, P])
        pre_scale = place("pre_scale", [P, T])
        post_scale = place("post_scale", [P, T])
        scratch = place("scratch", [P, 6 * T])
        warm = place("table_warmth", [P, 8])
        rec_const = place("rec_const", [P, 4, REC_TILES])
        soft = place("softplus_tmp", [P, 8, REC_TILES])
        f_base = top[0]
        f = place("f", [P, KD, T])
        hidden_base = top[0]
        hidden = place("hidden_hi_lo", [P, KF, 2 * T], F32R)
        hidden_end = top[0]
        assert hidden_end <= nc.sbuf_usable_end

        at = [f_base]
        gate_w = place("gate_weights", [P, REC_TILES, 2, P], at=at)
        mask = place("causal_mask", [P, 3 * P], at=at)
        ident = place("identity", [P, P], at=at)
        rope_t = place("rope_tables", [32, 2, T], at=at)
        rope_tmp = place("rope_tmp", [32, 2, T], at=at)
        v_rows = place("v_rows", [P, 2, P], at=at)
        assert at[0] <= hidden_base

        at = [hidden_base]
        merged = place("merged_hi_lo", [P, KD, 2 * T], F32R, at=at)
        squares = place("squares", [P, KD, T], at=[hidden_base])
        decay = place("decay", [P, REC_TILES, T], at=at)
        tanh_la = place("tanh_half_log_a", [P, REC_TILES, T], at=at)
        gated_in = place("gated_in", [P, REC_TILES, T], at=at)
        gelu = place("gelu", [P, REC_TILES, T], at=at)
        att = place("attention_out", [P, HEADS, T], at=at)
        xg = place("xr_and_gr", [P, 2, T + 4], at=at)
        half_norms = place("half_norms", [P, 2, T], at=[at[0]])
        conv = place("conv_out", [P, 2, T], at=at)
        gelu_tmp = place("gelu_tmp", [P, T], at=at)
        gate_t = place("gate_tanh", [P, 2, T], at=at)
        att_total = place("attention_squares", [P, T], at=[at[0]])
        q_rec = place("q_rec", [P, T], at=at)
        gate_w2 = place("gate_weights_now", [P, 2, 2, P], at=at)
        rec_sq = place("rec_square", [P, T], at=at)
        stat = place("softmax_stats", [P, 8], at=at)
        qkv = place("q_k_v", [P, 3, T], at=at)
        assert at[0] <= nc.sbuf_usable_end
        banks = ctx.enter_context(nc.psum_tensor("banks", [P, 8, 512], F32))

        params_loaded, ones_set = sem("params_loaded"), sem("ones_set")
        gates_loaded, mixer_loaded = sem("gates_loaded"), sem("mixer_loaded")
        x_loaded = [sem(f"x_loaded{i}") for i in range(4)]
        raw_loaded = [sem(f"raw_loaded{i}") for i in range(SLOTS)]
        hi_done, lo_done, piece_used = sem("hi_done"), sem("lo_done"), sem("piece_used")
        bank_read, evacuated, scaled = sem("bank_read"), sem("evacuated"), sem("scaled")
        fin_add = sem("fin_add")
        silu_done, gated, h_hi, h_lo = sem("silu_done"), sem("gated"), sem("h_hi"), sem("h_lo")
        sq_done, sq_summed, end_squared = sem("sq_done"), sem("sq_summed"), sem("end_squared")
        norm_summed, norm_root, norm_ready = sem("norm_summed"), sem("norm_root"), sem("norm_ready")
        f_gained = sem("f_gained")
        f_scaled, x_new, op_hi, op_lo = sem("f_scaled"), sem("x_new"), sem("op_hi"), sem("op_lo")
        x_squared, tree = sem("x_squared"), sem("tree")
        y_stored = sem("y_stored")
        pads_zero, conv0, conv_step, conv_done = sem("pads_zero"), sem("conv0"), sem("conv_step"), sem("conv_done")
        gr_squared, gelu_step, gelu_th, gelu_done = sem("gr_squared"), sem("gelu_step"), sem("gelu_th"), sem("gelu_done")
        gelu_mul, rec_den = sem("gelu_mul"), sem("rec_den")
        gatew_now, gates_done, gate_tanh, rec_step = sem("gatew_now"), sem("gates_done"), sem("gate_tanh"), sem("rec_step")
        soft_step, soft_act = sem("soft_step"), sem("soft_act")
        root_t, u_done, scan_step, rec_done = sem("root_t"), sem("u_done"), sem("scan_step"), sem("rec_done")
        rec_sqd, rec_sum = sem("rec_sqd"), sem("rec_sum")
        rec_made, rec_lo, att_made, att_lo = sem("rec_made"), sem("rec_lo"), sem("att_made"), sem("att_lo")
        rope_step, scored, softmax_step, exp_done = (
            sem("rope_step"), sem("scored"), sem("softmax_step"), sem("exp_done"))
        v_turned, v_copied, p_ready, p_turned, p_copied = (
            sem("v_turned"), sem("v_copied"), sem("p_ready"), sem("p_turned"), sem("p_copied"))
        rec_scaled, att_scaled, halves_added = sem("rec_scaled"), sem("att_scaled"), sem("halves_added")
        pv_done, att_sqd, att_sum = sem("pv_done"), sem("att_sqd"), sem("att_sum")

        t2 = scratch[:, 0:2 * T].rearrange("p (i t) -> p i t", i=2)
        gu = scratch[:, 2 * T:4 * T].rearrange("p (i t) -> p i t", i=2)
        sg = scratch[:, 4 * T:5 * T]
        sq = scratch[:, 5 * T:6 * T]
        sq_end = scratch[:, 2 * T:4 * T].rearrange("p (i t) -> p i t", i=2)
        t3 = scratch[:, 0:3 * T].rearrange("p (i t) -> p i t", i=3)
        prob = scratch[:, 3 * T:3 * T + 3 * P]
        prob_t = scratch[:, 3 * T + 3 * P:3 * T + 6 * P]

        def both(ap, n=2):
            return ap.unsqueeze(1).to_broadcast([ap.shape[0], n, T])

        def size_of(n_static):
            for first in (DOWN1, DOWN2):
                if first <= n_static < first + DOWN_PIECES * KD:
                    j = (n_static - first) % DOWN_PIECES
                    return P * (min(KF, PIECE * (j + 1)) - PIECE * j)
            return P * PIECE

        def by_vector(k):
            return k // 2 % 3 == 1

        def scalings(n, k):
            return n * (KD // 2 + 1) + (k if k < 2 else k // 2 + 1) + 1

        block = ctx.enter_context(nc.Block())

        @block.sync
        def _(sp):
            def load(n, s, src):
                if s >= SLOTS:
                    sp.wait_ge(lo_done, n - (SLOTS - 1))
                sp.dma_start(raw[:, s % SLOTS, 0:size_of(s)], src).then_inc(raw_loaded[s % SLOTS], 16)

            def load_quad(w, base, between=lambda j: None):
                for j in range(8):
                    kh, i = divmod(j, 4)
                    load(base + j, base + j, w[i, :, kh * PIECE * P:(kh + 1) * PIECE * P])
                    between(j)

            def mixer_table(i):
                if i == 0:
                    sp.wait_ge(pads_zero, 2)
                if i < 4:
                    half, g = divmod(i, 2)
                    sp.dma_start(gate_w[64 * half:64 * half + 64, :, g, 64 * half:64 * half + 64], gates[g, half])\
                        .then_inc(gates_loaded, 16)
                if i == 4:
                    sp.dma_start(mask[:, :], consts[:, 0:3 * P]).then_inc(mixer_loaded, 16)
                if i == 5:
                    sp.dma_start(ident[:, :], consts[:, 3 * P:4 * P]).then_inc(mixer_loaded, 16)
                if i == 6:
                    sp.dma_start(rope_t[:, :, :], rope).then_inc(mixer_loaded, 16)

            def load_groups(w, base, count, per, peel, unroll, after=lambda i: None):
                for g, s in tiles(sp, count, peel, unroll):
                    if peel and s < 2:
                        continue
                    for kh in range(2):
                        for i in range(per):
                            j = kh * per + i
                            src = w[bass.ds(g * per + i, 1), :, kh * PIECE * P:(kh + 1) * PIECE * P]
                            load(g * (2 * per) + (base + j), s * 2 * per + base + j,
                                 src.rearrange("a p c -> p (a c)"))
                            if s < 4:
                                after(4 * (s - 2) + j)

            def load_down(w, base):
                for d, s in tiles(sp, KD, 0, 2):
                    for j in range(DOWN_PIECES):
                        a = base + s * DOWN_PIECES + j
                        src = w[bass.ds(d, 1), :, j * PIECE * P:j * PIECE * P + size_of(a)]
                        load(d * DOWN_PIECES + (base + j), a, src.rearrange("a p c -> p (a c)"))

            def load_x(c):
                sp.dma_start(xs[:, 4 * c:4 * c + 4, :], x[:, 4 * c:4 * c + 4, :]).then_inc(x_loaded[c], 16)

            load_quad(up1, UP1, lambda j: load_x(j) if j < 4 else None)
            load_groups(up1, UP1, KF, 2, 2, 2)
            load_down(down1, DOWN1)
            load_quad(rec_in, REC)
            load_groups(rec_in, REC, REC_TILES, 2, 4, 2, mixer_table)
            load_groups(att_in, ATT, HEADS, 3, 0, 2)
            load_groups(out_w, OUT, KD // 4, 4, 0, 1)
            load_quad(up2, UP2)
            load_groups(up2, UP2, KF, 2, 2, 2)
            load_down(down2, DOWN2)
            for k in [*range(0, KD - 4, 2), KD - 2, KD - 4]:
                if by_vector(k):
                    sp.wait_ge(fin_add, sum(map(by_vector, range(0, k + 1, 2))))
                else:
                    sp.wait_ge(x_new, 2 * KD + sum(not by_vector(i) for i in range(k + 2)))
                sp.dma_start(y[:, k:k + 2, :], xs[:, k:k + 2, :]).then_inc(y_stored, 16)
            sp.wait_ge(y_stored, 16 * KD // 2)

        @block.tensor
        def _(pe):
            def piece(n, s, bank, k0, moving, first, last, k_ready=None, one_half=False):
                pe.wait_ge(lo_done, n + 1)
                for kk in range(size_of(s) // P):
                    k = k0 + kk
                    if k_ready is not None:
                        k_ready(k)
                    cols = slice(kk * P, (kk + 1) * P)
                    if one_half:
                        nc.tensor.matmul(banks[:, bank, 0:T], w_hi[:, s % SLOTS, cols], moving[:, k, 0:T],
                                         start=first and kk == 0, stop=False)
                        nc.tensor.matmul(banks[:, bank, 0:T], w_hi[:, s % SLOTS, cols], moving[:, k, T:2 * T],
                                         start=False, stop=False)
                    else:
                        nc.tensor.matmul(banks[:, bank, :], w_hi[:, s % SLOTS, cols], moving[:, k, :],
                                         start=first and kk == 0, stop=False)
                    mm = nc.tensor.matmul(banks[:, bank, 0:T], w_lo[:, s % SLOTS, cols], moving[:, k, 0:T],
                                          start=False, stop=last and kk == size_of(s) // P - 1)
                mm.then_inc(piece_used, 1)

            def quad(base, first_bank, n_op):
                for kk in range(PIECE if n_op else 0):
                    for i in range(2):
                        if kk == 0:
                            pe.wait_ge(lo_done, base + i + 1)
                        pe.wait_ge(op_lo, n_op + kk + 1)
                        cols = slice(kk * P, (kk + 1) * P)
                        bank = (first_bank + i) % 4
                        nc.tensor.matmul(banks[:, bank, :], w_hi[:, i, cols], operand[:, kk, :],
                                         start=kk == 0, stop=False)
                        mm = nc.tensor.matmul(banks[:, bank, 0:T], w_lo[:, i, cols], operand[:, kk, 0:T],
                                              start=False, stop=False)
                        if kk == PIECE - 1:
                            mm.then_inc(piece_used, 1)
                for j in range(2 if n_op else 0, 8):
                    kh, i = divmod(j, 4)
                    piece(base + j, base + j, (first_bank + i) % 4, kh * PIECE, operand, kh == 0, kh == 1,
                          (lambda k: pe.wait_ge(op_lo, n_op + k + 1)) if i == 0 else None)

            def group(g, s, base, bank):
                for j in range(4):
                    kh, i = divmod(j, 2)
                    piece(g * 4 + (base + j), s * 4 + base + j, bank + i, kh * PIECE, operand, kh == 0, kh == 1)

            def token_sums(values, wait_sem, wait_value):
                pe.wait_ge(wait_sem, wait_value)
                nc.tensor.matmul(banks[:, 5, 0:T], ones[:, :], values, start=True, stop=True).then_inc(norm_summed, 1)

            def post_sums(n_sq, g_last):
                pe.wait_ge(sq_summed, n_sq + KD - 1)
                nc.tensor.matmul(banks[:, 5, 0:T], ones[:, :], post_scale[:, :], start=True, stop=False)
                pe.wait_ge(bank_read, g_last + 1)
                nc.tensor.matmul(banks[:, 5, 0:T], ones[:, :], sq, start=False, stop=True).then_inc(norm_summed, 1)

            def ffn(up_base, down_base, g_up, g_down, norms, n_op, n_h):
                quad(up_base, 0, n_op)
                token_sums(squares[:, 0, :], tree, 5 * (norms + 1))
                for g, s in tiles(pe, KF, 2, 2):
                    if s >= 2:
                        pe.wait_ge(evacuated, g + (g_up - 1))
                        group(g, s, up_base, 2 * (s % 2))
                for d, s in tiles(pe, KD, 4, 4, tail=1):
                    if s < 2:
                        pe.wait_ge(evacuated, g_up + KF - 1)
                    elif s < 4:
                        pe.wait_ge(evacuated, g_up + KF)
                    else:
                        pe.wait_ge(evacuated, d + (g_down - 3))
                    for j in range(DOWN_PIECES):
                        a = down_base + s * DOWN_PIECES + j
                        ready = (lambda k: pe.wait_ge(h_lo, n_h + k + 1)) if s == 0 else None
                        piece(d * DOWN_PIECES + (down_base + j), a, (s + 2) % 4, PIECE * j, hidden,
                              j == 0, j == DOWN_PIECES - 1, ready, one_half=s == KD - 1)
                post_sums(N_SQ[norms], g_down + KD - 1)

            pe.wait_ge(ones_set, 1)
            ffn(UP1, DOWN1, G_UP1, G_DOWN1, 0, 0, 0)

            def gate_products(n, s):
                pe.wait_ge(conv_done, n + 1)
                pe.wait_ge(gatew_now, n + 1)
                if s >= 1:
                    pe.wait_ge(gate_tanh, 3 * n)
                nc.tensor.matmul(banks[:, 6, 0:T], gate_w2[:, s % 2, 0, :], conv[:, s % 2, :], start=True, stop=True)
                nc.tensor.matmul(banks[:, 6, T:2 * T], gate_w2[:, s % 2, 1, :], conv[:, s % 2, :],
                                 start=True, stop=True).then_inc(gates_done, 1)

            quad(REC, 2, KD)
            token_sums(squares[:, 0, :], tree, 10)
            for g, s in tiles(pe, REC_TILES, 4, 2):
                if s >= 2:
                    pe.wait_ge(evacuated, g + (G_REC - 1))
                    group(g, s, REC, 2 * ((s + 1) % 2))
                    gate_products(g - 2, s - 2)

            def scores(h, s):
                pe.wait_ge(rope_step, h * 4 + 4)
                if s >= 1:
                    pe.wait_ge(p_copied, h)
                else:
                    pe.wait_ge(gate_tanh, 3 * REC_TILES)
                q, k = qkv[:, 0, :], qkv[:, 1, :]
                nc.tensor.matmul(banks[:, 6, 0:P], q[:, 0:P], k[:, 0:P], start=True, stop=True)
                nc.tensor.matmul(banks[:, 6, P:2 * P], q[:, P:T], k[:, P:T], start=True, stop=True)
                nc.tensor.matmul(banks[:, 6, 2 * P:3 * P], q[:, P:T], k[:, 0:P], start=True, stop=True)\
                    .then_inc(scored, 1)

            def turn_v(h, s):
                pe.wait_ge(rope_step, h * 4 + 4)
                if s >= 1:
                    pe.wait_ge(v_copied, h)
                    pe.wait_ge(att_made, h * 2)
                pe.wait_ge(mixer_loaded, 3 * 16)
                nc.tensor.transpose(banks[:, 7, 0:P], qkv[:, 2, 0:P], ident[:, :])
                nc.tensor.transpose(banks[:, 7, P:2 * P], qkv[:, 2, P:T], ident[:, :]).then_inc(v_turned, 1)

            def turn_probs(h):
                pe.wait_ge(p_ready, h * 2 + 2)
                nc.tensor.transpose(banks[:, 6, 0:P], prob[:, 0:P], ident[:, :])
                nc.tensor.transpose(banks[:, 6, P:2 * P], prob[:, 2 * P:3 * P], ident[:, :])
                nc.tensor.transpose(banks[:, 6, 2 * P:3 * P], prob[:, P:2 * P], ident[:, :]).then_inc(p_turned, 1)

            def weighted_v(h):
                pe.wait_ge(v_copied, h + 1)
                pe.wait_ge(p_copied, h + 1)
                nc.tensor.matmul(banks[:, 7, T:2 * T], v_rows[:, 0, :], prob_t[:, 0:T], start=True, stop=False)
                nc.tensor.matmul(banks[:, 7, T + P:2 * T], v_rows[:, 1, :], prob_t[:, T:T + P],
                                 start=False, stop=True).then_inc(pv_done, 1)

            for h, s in tiles(pe, HEADS, 4, 2, tail=2):
                b0 = 3 * ((s + 1) % 2)
                if s >= 1:
                    pe.wait_ge(evacuated, h + (G_ATT - 1))
                else:
                    pe.wait_ge(evacuated, G_ATT - 1)
                for j in range(6):
                    kh, i = divmod(j, 3)
                    piece(h * 6 + (ATT + j), ATT + s * 6 + j, b0 + i, kh * PIECE, operand, kh == 0, kh == 1)
                    if s == 0 and j == 1 or s == 1 and j == 0:
                        gate_products(REC_TILES - 2 + s, REC_TILES - 2 + s)
                    if s >= 2 and j == 1:
                        turn_probs(h - 2)
                    if s >= 2 and j == 2:
                        weighted_v(h - 2)
                    if s >= 1 and j == 3:
                        scores(h - 1, s - 1)
                        turn_v(h - 1, s - 1)
                    if s == HEADS - 1 and j == 1:
                        pe.wait_ge(evacuated, G_ATT + HEADS - 1)
                        token_sums(post_scale[:, :], rec_sum, REC_TILES)

            def out_piece(g, s, j, ready=None):
                if s >= 1 or j >= 4:
                    pe.wait_ge(evacuated, g * 8 + (G_OUT - 3 + j))
                kh, i = divmod(j, 4)
                piece(g * 8 + (OUT + j), OUT + s * 8 + j, OUT_BANKS[i], kh * PIECE, merged, True, True,
                      ready, one_half=s == KD // 4 - 1 and j == 7)

            last = HEADS - 1

            def att_ready(k):
                if k == PIECE + 2:
                    weighted_v(last)
                pe.wait_ge(att_lo, k - PIECE + 1)

            pe.wait_ge(rec_lo, REC_TILES)
            out_piece(0, 0, 0)
            turn_probs(last - 1)
            out_piece(0, 0, 1)
            scores(last, last)
            weighted_v(last - 1)
            pe.wait_ge(evacuated, G_ATT + HEADS)
            out_piece(0, 0, 2)
            turn_v(last, last)
            out_piece(0, 0, 3)
            turn_probs(last)
            out_piece(0, 0, 4, att_ready)
            pe.wait_ge(norm_root, 4)
            token_sums(pre_scale[:, :], att_sum, HEADS)
            out_piece(0, 0, 5)
            out_piece(0, 0, 6)
            out_piece(0, 0, 7)
            for g, s in tiles(pe, KD // 4, 1, 1, tail=1):
                if s >= 1:
                    for j in range(8):
                        out_piece(g, s, j)
            pe.wait_ge(sq_summed, 2 * KD - 3)
            nc.tensor.matmul(banks[:, 5, 0:T], ones[:, :], post_scale[:, :], start=True, stop=False)
            pe.wait_ge(end_squared, 1)
            nc.tensor.matmul(banks[:, 5, 0:T], ones[:, :], sq_end[:, 0, :], start=False, stop=False)
            pe.wait_ge(bank_read, G_UP2)
            nc.tensor.matmul(banks[:, 5, 0:T], ones[:, :], sq_end[:, 1, :], start=False, stop=True)\
                .then_inc(norm_summed, 1)
            ffn(UP2, DOWN2, G_UP2, G_DOWN2, 2, 2 * KD, KF)

        @block.scalar
        def _(act):
            def split_hi(n, s):
                act.wait_ge(raw_loaded[s % SLOTS], n * 4 + (16 - 4 * (s % SLOTS)))
                if s >= SLOTS:
                    act.wait_ge(piece_used, n - (SLOTS - 1))
                cols = slice(0, size_of(s))
                nc.scalar.copy(w_hi[:, s % SLOTS, cols], raw[:, s % SLOTS, cols]).then_inc(hi_done, 1)

            def right(pieces, e, bank, n, dst):
                act.wait_ge(piece_used, pieces)
                act.wait_ge(evacuated, e)
                nc.scalar.copy(dst, banks[:, bank:bank + n, T:2 * T]).then_inc(bank_read, 1)

            def silu(n, s, n_h):
                act.wait_ge(scaled, n + (1 + (0 if n_h == 0 else KF + REC_TILES + HEADS)))
                if s >= 1 or n_h:
                    act.wait_ge(h_lo, n + n_h)
                nc.scalar.activation(sg, gu[:, 0, :], ACT.Silu).then_inc(silu_done, 1)

            def hidden_hi(n, n_h):
                act.wait_ge(gated, n + (n_h + 1))
                nc.scalar.copy(hidden[:, bass.ds(n, 1), 0:T].rearrange("p a t -> p (a t)"), sg).then_inc(h_hi, 1)

            def root(m, dst, scale, eps_col):
                act.wait_ge(norm_summed, m + 1)
                nc.scalar.activation(dst, banks[:, 5, 0:T], ACT.Sqrt, bias=param[:, C_EPS + eps_col:C_EPS + eps_col + 1],
                                     scale=scale).then_inc(norm_root, 1)

            def square_f(d, s, e, n_sq):
                if e is not None:
                    act.wait_ge(evacuated, e + 1)
                if s >= 1 or n_sq:
                    act.wait_ge(sq_summed, d + n_sq)
                nc.scalar.activation(sq, f[:, bass.ds(d, 1), :].rearrange("p a t -> p (a t)"),
                                     ACT.Square).then_inc(sq_done, 1)

            def operand_hi(gain, updated, nxt=None):
                for k in range(KD):
                    if updated is None:
                        if k % 4 == 0:
                            split_hi(k // 4, k // 4)
                            if k == 0:
                                act.wait_ge(params_loaded, 16)
                            act.wait_ge(x_loaded[k // 4], 16)
                    else:
                        act.wait_ge(x_new, updated + k + 1)
                    nc.scalar.mul(operand[:, k, 0:T], xs[:, k, :], param[:, gain + k:gain + k + 1]).then_inc(op_hi, 1)
                    if updated is not None and k == UPDATE_HI:
                        split_hi(nxt + 4, nxt + 4)

            def x_squares(half):
                for c in (2 * half, 2 * half + 1):
                    nc.scalar.activation(squares[:, 4 * c:4 * c + 4, :], xs[:, 4 * c:4 * c + 4, :],
                                         ACT.Square).then_inc(x_squared, 1)

            def warm_sqrt(n):
                nc.scalar.activation(warm[:, n:n + 1], param[:, C_EPS:C_EPS + 1], ACT.Sqrt)

            def square_last(pieces, e, bank, phase):
                act.wait_ge(piece_used, pieces)
                act.wait_ge(sq_summed, N_SQ[phase] + KD - 1)
                nc.scalar.activation(sq, banks[:, bank, 0:T], ACT.Square).then_inc(bank_read, 1)

            def gain_f(d, post_gain, n_sq):
                act.wait_ge(sq_done, d + (n_sq + 1))
                tile = f[:, bass.ds(d, 1), :].rearrange("p a t -> p (a t)")
                nc.scalar.mul(tile, tile, param[:, bass.ds(d + post_gain, 1)]).then_inc(f_gained, 1)

            def ffn(up_base, down_base, g_up, g_down, m, gain, updated, post_gain, n_h, n_sq,
                    beside_down=lambda: None):
                operand_hi(gain, updated, up_base)
                for n, s in tiles(act, KF, 4, 2):
                    for j in range(4):
                        if s and not (n_h and s == 1 and j == 0):
                            split_hi(n * 4 + (up_base + j), up_base + 4 * s + j)
                        if s == 1 and j < 2:
                            x_squares(j)
                        if s >= 3 and j == 0:
                            silu(n - 2, s - 2, n_h)
                        if s >= 3 and j == 1:
                            hidden_hi(n - 2, n_h)
                    if s == 2:
                        root(m, pre_scale[:, :], 1.0 / D, 0)
                        silu(0, 0, n_h)
                        hidden_hi(0, n_h)
                    if s >= 1:
                        right(up_base + 6 if s == 1 else n * 4 + up_base, n + (g_up - 1), 2 * ((s - 1) % 2), 2, t2)
                for j in range(4):
                    split_hi(down_base + j, down_base + j)
                    if j == 0:
                        silu(KF - 2, KF - 2, n_h)
                    if j == 1:
                        hidden_hi(KF - 2, n_h)
                right(down_base, g_up + KF - 1, 2 * ((KF - 1) % 2), 2, t2)
                silu(KF - 1, KF - 1, n_h)
                hidden_hi(KF - 1, n_h)
                for d, s in tiles(act, KD, 4, 4):
                    for j in range(DOWN_PIECES):
                        if not (s == 0 and j < 4):
                            split_hi(d * DOWN_PIECES + (down_base + j), down_base + s * DOWN_PIECES + j)
                        if s >= 1 and j == 3:
                            right(d * DOWN_PIECES + down_base, d + (g_down - 1), (s + 1) % 4, 1, t2[:, 0:1, :])
                        if s >= 1 and j == 4:
                            square_f(d - 1, s - 1, d + (g_down - 1), n_sq)
                        if s >= 1 and j == 5:
                            gain_f(d - 1, post_gain, n_sq)
                        if s == 2 and j == 0:
                            beside_down()

            def after_down(nxt, g_down, phase, m, scale, eps_col, post_gain):
                warm_sqrt(m)
                if nxt is not None:
                    for j in range(3):
                        split_hi(nxt + j, nxt + j)
                square_last(END if nxt is None else nxt, g_down + KD - 1, (KD + 1) % 4, phase)
                root(m, post_scale[:, :], scale, eps_col)
                last = post_gain + KD - 1
                nc.scalar.mul(f[:, KD - 1, :], banks[:, (KD + 1) % 4, 0:T], param[:, last:last + 1])\
                    .then_inc(evacuated, 1)
                if nxt is not None:
                    split_hi(nxt + 3, nxt + 3)

            act.dma_start(param[:, :], params).then_inc(params_loaded, 16)
            lam = param[:, C_LAM:C_LAM + REC_TILES]

            def soft_exp():
                nc.scalar.activation(soft[:, 0, :], lam, ACT.Abs).then_inc(soft_act, 1)
                act.wait_ge(soft_act, 1)
                nc.scalar.activation(soft[:, 1, :], soft[:, 0, :], ACT.Exp, scale=-1.0).then_inc(soft_act, 1)

            ffn(UP1, DOWN1, G_UP1, G_DOWN1, 0, C_FFN1_PRE, None, C_FFN1_POST, 0, 0, soft_exp)
            after_down(REC, G_DOWN1, 0, 1, 4.0 / D, 1, C_FFN1_POST)

            operand_hi(C_MIX_PRE, 0, REC)

            def conv_first(n, s):
                act.wait_ge(scaled, n + (KF + 1))
                if s >= 2:
                    act.wait_ge(gates_done, n - 1)
                    act.wait_ge(rec_step, n * 5 - 5)
                col = lambda c: param[:, bass.ds(n + c, 1)]
                nc.scalar.activation(conv[:, s % 2, :], xg[:, 0, 1:T + 1], ACT.Identity,
                                     bias=col(C_CONV_B), scale=col(C_CONV_W)).then_inc(conv0, 1)

            def gr_square(n, s):
                if s >= 1:
                    act.wait_ge(gelu_done, n)
                nc.scalar.activation(gelu_tmp[:, :], xg[:, 1, 4:T + 4], ACT.Square).then_inc(gr_squared, 1)

            def gelu_tanh(n):
                act.wait_ge(gelu_step, n * 2 + 2)
                nc.scalar.activation(gelu_tmp[:, :], gelu_tmp[:, :], ACT.Tanh, scale=GELU_S).then_inc(gelu_th, 1)

            def gate_tanhs(n, s):
                act.wait_ge(gates_done, n + 1)
                if s == 0:
                    act.wait_ge(soft_step, 15)
                if s >= 1:
                    act.wait_ge(rec_step, n * 5)
                const = lambda c: rec_const[:, c, bass.ds(n, 1)]
                nc.scalar.activation(gate_t[:, 0, :], banks[:, 6, 0:T], ACT.Tanh, bias=const(0), scale=0.5)\
                    .then_inc(gate_tanh, 1)
                nc.scalar.activation(gate_t[:, 1, :], banks[:, 6, T:2 * T], ACT.Tanh, bias=const(1), scale=0.5)\
                    .then_inc(gate_tanh, 1)
                act.wait_ge(gate_tanh, n * 3 + 2)
                nc.scalar.activation(tanh_la[:, bass.ds(n, 1), :].rearrange("p a t -> p (a t)"), gate_t[:, 0, :],
                                     ACT.Tanh, bias=const(2), scale=const(2)).then_inc(gate_tanh, 1)

            def rec_stages(n, s, j):
                if j == 0 and 2 <= s < REC_TILES + 2:
                    conv_first(n - 2, s - 2)
                    gr_square(n - 2, s - 2)
                if j == 1 and 2 <= s < REC_TILES + 2:
                    gelu_tanh(n - 2)
                if j == 3 and 3 <= s < REC_TILES + 3:
                    gate_tanhs(n - 3, s - 3)

            for n, s in tiles(act, REC_TILES, 4, 2):
                for j in range(4):
                    if s and not (s == 1 and j == 0):
                        split_hi(n * 4 + (REC + j), REC + 4 * s + j)
                    if s == 1 and j < 2:
                        x_squares(j)
                    if s != 2:
                        rec_stages(n, s, j)
                if s == 2:
                    root(2, pre_scale[:, :], 1.0 / D, 0)
                    rec_stages(2, 2, 0)
                    rec_stages(2, 2, 1)
                if s >= 1:
                    right(REC + 6 if s == 1 else n * 4 + REC, n + (G_REC - 1), 2 * (s % 2), 2, t2)

            def softmax_exp(h):
                act.wait_ge(softmax_step, 4 * h + 4)
                scale = P ** -0.5
                nc.scalar.activation(prob[:, 0:P], prob[:, 0:P], ACT.Exp, bias=stat[:, 2:3], scale=scale,
                                     accum_out=stat[:, 4:5]).then_inc(exp_done, 1)
                nc.scalar.activation(prob[:, P:3 * P], prob[:, P:3 * P], ACT.Exp, bias=stat[:, 3:4], scale=scale,
                                     accum_out=stat[:, 5:6]).then_inc(exp_done, 1)

            def copy_v(h):
                act.wait_ge(v_turned, h + 1)
                if h >= 1:
                    act.wait_ge(pv_done, h)
                nc.scalar.copy(v_rows[:, :, :].rearrange("p a t -> p (a t)"), banks[:, 7, 0:T]).then_inc(v_copied, 1)

            def copy_probs(h):
                act.wait_ge(p_turned, h + 1)
                nc.scalar.copy(prob_t, banks[:, 6, 0:3 * P]).then_inc(p_copied, 1)

            def operand_halves(source, h, gain, k, gained, made):
                scale = param[:, gain + h:gain + h + 1]
                nc.scalar.mul(merged[:, k, 0:T], source, scale).then_inc(made, 1)
                nc.scalar.mul(gained[:, h, :], source, scale).then_inc(made, 1)

            def take_att(h):
                act.wait_ge(pv_done, h + 1)
                if h >= 1:
                    act.wait_ge(att_sum, h)
                else:
                    act.wait_ge(gelu_done, REC_TILES)
                if h < HEADS - 1:
                    nc.scalar.activation(squares_att, banks[:, 7, T:2 * T], ACT.Square).then_inc(att_sqd, 1)
                operand_halves(banks[:, 7, T:2 * T], h, C_ATT_OUT, PIECE + h, att, att_made)
                if h == HEADS - 1:
                    nc.scalar.activation(squares_att, banks[:, 7, T:2 * T], ACT.Square).then_inc(att_sqd, 1)

            squares_att = gelu_tmp[:, :]

            def root_tanh():
                act.wait_ge(gate_tanh, 3 * REC_TILES)
                nc.scalar.activation(tanh_la[:, :, :], tanh_la[:, :, :], ACT.Sqrt).then_inc(root_t, 1)

            def rec_square(j):
                act.wait_ge(rec_done, j + 1)
                if j >= 1:
                    act.wait_ge(rec_sum, j)
                nc.scalar.activation(rec_sq[:, :], gated_in[:, j, :], ACT.Square).then_inc(rec_sqd, 1)
                operand_halves(gated_in[:, j, :], j, C_REC_OUT, j, gelu, rec_made)

            for h in range(HEADS + 1):
                base = ATT + 6 * h
                for j in range(6 if h < HEADS else 4):
                    if h == HEADS and j == 3:
                        right(base, G_ATT + h - 1, 3 * (h % 2), 3, t3)
                    split_hi(base + j, base + j)
                    if h >= 3 and j == 0:
                        take_att(h - 3)
                    if h < 2 and j < 2:
                        rec_stages(REC_TILES + h, REC_TILES + h, j)
                    if h < 2 and j == 5:
                        gate_tanhs(REC_TILES - 2 + h, REC_TILES - 2 + h)
                    if h >= 2 and j == 1:
                        copy_v(h - 2)
                    if h >= 2 and j == (2 if h < HEADS else 1):
                        softmax_exp(h - 2)
                    if j == 3 and h == 0:
                        right(ATT, G_ATT - 1, 2 * (REC_TILES % 2), 2, t2)
                        rec_stages(REC_TILES, REC_TILES, 3)
                    if j == 3 and 1 <= h < HEADS:
                        right(base, G_ATT + h - 1, 3 * (h % 2), 3, t3)
                    if j == 4 and h >= 2:
                        copy_probs(h - 2)
                    if h == 3 and j == 0:
                        root_tanh()
                    if 3 <= h <= 6 and j == 4:
                        rec_square(2 * (h - 3))
                    if 4 <= h <= 7 and j == 1:
                        rec_square(2 * (h - 4) + 1)

            def out_right(n, s):
                right(n + (OUT + 1), n + G_OUT, OUT_BANKS[s % 4], 1, t2[:, 0:1, :])

            copy_probs(HEADS - 2)
            split_hi(OUT + 4, OUT + 4)
            out_right(0, 0)
            take_att(HEADS - 2)
            softmax_exp(HEADS - 1)
            warm_sqrt(0)
            root(3, half_norms[:, 0, :], 1.0 / (REC_TILES * P), 0)
            out_right(1, 1)
            split_hi(OUT + 5, OUT + 5)
            copy_v(HEADS - 1)
            out_right(2, 2)
            split_hi(OUT + 6, OUT + 6)
            copy_probs(HEADS - 1)
            take_att(HEADS - 1)
            out_right(3, 3)
            split_hi(OUT + 7, OUT + 7)

            for g, s in tiles(act, KD // 4 - 1, 1, 1):
                for j in range(8):
                    out_right(g * 8 + (4 + j), 4 + j)
                    split_hi(g * 8 + (OUT + 8 + j), OUT + 8 + s * 8 + j)
                    if s == 0 and j == 0:
                        root(4, half_norms[:, 1, :], 1.0 / (HEADS * P), 0)
                    if j < 4:
                        act.wait_ge(halves_added, g * 4 + (j + 1))
                        square_f(g * 4 + j, s * 4 + j, None, KD - 1)
                    else:
                        gain_f(g * 4 + (j - 4), C_MIX_POST, KD - 1)
            warm_sqrt(5)
            for j in range(2):
                out_right(2 * KD - 4 + j, j)
                split_hi(UP2 + j, UP2 + j)
                act.wait_ge(halves_added, KD - 3 + j)
                square_f(KD - 4 + j, KD - 4 + j, None, KD - 1)
            out_right(2 * KD - 2, 2)
            split_hi(UP2 + 2, UP2 + 2)
            act.wait_ge(halves_added, KD - 1)
            nc.scalar.activation(sq_end[:, 0, :], f[:, KD - 2, :], ACT.Square).then_inc(end_squared, 1)
            act.wait_ge(halves_added, KD)
            nc.scalar.activation(sq_end[:, 1, :], f[:, KD - 1, :], ACT.Square).then_inc(bank_read, 1)
            root(5, post_scale[:, :], 1.0 / D, 0)
            act.wait_ge(sq_done, N_SQ[2])
            act.wait_ge(end_squared, 1)
            act.wait_ge(bank_read, G_UP2)
            for k in range(KD - 4, KD):
                nc.scalar.mul(f[:, k, :], f[:, k, :], param[:, C_MIX_POST + k:C_MIX_POST + k + 1]).then_inc(f_gained, 1)
            split_hi(UP2 + 3, UP2 + 3)
            ffn(UP2, DOWN2, G_UP2, G_DOWN2, 6, C_FFN2_PRE, KD, C_FFN2_POST, KF, N_SQ[2])
            after_down(None, G_DOWN2, 2, 7, 4.0 / D, 1, C_FFN2_POST)

        @block.vector
        def _(dve):
            v = nc.vector

            def split_lo(n, s):
                dve.wait_ge(hi_done, n + 1)
                cols = slice(0, size_of(s))
                v.tensor_tensor(w_lo[:, s % SLOTS, cols], raw[:, s % SLOTS, cols],
                                w_hi[:, s % SLOTS, cols].bitcast(F32), ALU.subtract).then_inc(lo_done, 1)

            def add_halves(e, bank, n, src, dst):
                dve.wait_ge(bank_read, e + 1)
                v.tensor_tensor(dst, banks[:, bank:bank + n, 0:T], src, ALU.add).then_inc(evacuated, 1)

            def scale_tokens(e, ap, n):
                dve.wait_ge(evacuated, e + 1)
                v.tensor_tensor(ap, ap, both(pre_scale[:, :], n), ALU.mult).then_inc(scaled, 1)

            def gate_hidden(n, n_h):
                dve.wait_ge(silu_done, n + (n_h + 1))
                v.tensor_tensor(sg, sg, gu[:, 1, :], ALU.mult).then_inc(gated, 1)

            def hidden_lo(n, n_h):
                dve.wait_ge(h_hi, n + (n_h + 1))
                col = bass.ds(n, 1)
                v.tensor_tensor(hidden[:, col, T:2 * T].rearrange("p a t -> p (a t)"), sg,
                                hidden[:, col, 0:T].rearrange("p a t -> p (a t)").bitcast(F32), ALU.subtract)\
                    .then_inc(h_lo, 1)

            def inverse(m, ap):
                dve.wait_ge(norm_root, m + 1)
                v.reciprocal(ap, ap).then_inc(norm_ready, 1)

            def add_square(d, s, n_sq):
                dve.wait_ge(sq_done, d + (n_sq + 1))
                if s == 0:
                    v.tensor_copy(post_scale[:, :], sq).then_inc(sq_summed, 1)
                else:
                    dve.wait_ge(sq_summed, d + n_sq)
                    v.tensor_tensor(post_scale[:, :], post_scale[:, :], sq, ALU.add).then_inc(sq_summed, 1)

            def update_x(m, n, pre_gain, n_op, between=lambda k: None):
                dve.wait_ge(norm_ready, m + 1)
                for k in range(KD + 3):
                    width = 1 if k < 2 else 2
                    if k < KD and k % width == 0:
                        if k == KD - 2:
                            dve.wait_ge(evacuated, (G_REC, G_UP2, G_DOWN2 + KD)[n])
                        dve.wait_ge(f_gained, min(GAINED[n] + k + width, GAINED[n + 1]))
                        v.tensor_tensor(f[:, k:k + width, :], f[:, k:k + width, :], both(post_scale[:, :], width),
                                        ALU.mult).then_inc(f_scaled, 1)
                    if k >= 3 and pre_gain is not None:
                        operand_lo(k - 3, pre_gain, n_op)
                    between(k)
                    own = k - 2
                    if own >= 0 and own % 2 == 0 and own < KD and pre_gain is None and by_vector(own):
                        dve.wait_ge(f_scaled, scalings(n, own))
                        v.tensor_tensor(xs[:, own:own + 2, :], xs[:, own:own + 2, :], f[:, own:own + 2, :], ALU.add)\
                            .then_inc(fin_add, 1)

            def operand_lo(k, pre_gain, n_op):
                dve.wait_ge(op_hi, n_op + k + 1)
                v.scalar_tensor_tensor(operand[:, k, T:2 * T], xs[:, k, :], param[:, pre_gain + k:pre_gain + k + 1],
                                       operand[:, k, 0:T].bitcast(F32), ALU.mult, ALU.subtract).then_inc(op_lo, 1)

            def pre_inverse(m):
                inverse(m, pre_scale[:, :])
                dve.wait_ge(norm_ready, m + 1)

            def ffn(up_base, down_base, g_up, g_down, m, n_h, n_sq, beside_down=lambda: None):
                for n, s in tiles(dve, KF, 4, 2):
                    for j in range(4):
                        if s >= 2 and j == 0:
                            add_halves(n + (g_up - 2), 2 * (s % 2), 2, t2, gu)
                        if s >= 3 and j == 0:
                            scale_tokens(n + (g_up - 2), gu, 2)
                        if s and not (n_h and s == 1 and j == 0):
                            split_lo(n * 4 + (up_base + j), up_base + 4 * s + j)
                        if s >= 3 and j == 0:
                            gate_hidden(n - 2, n_h)
                        if s >= 3 and j == 1:
                            hidden_lo(n - 2, n_h)
                    if s == 2:
                        pre_inverse(m)
                        scale_tokens(g_up, gu, 2)
                        gate_hidden(0, n_h)
                        hidden_lo(0, n_h)
                for j in range(4):
                    if j == 0:
                        add_halves(g_up + KF - 2, 2 * ((KF - 2) % 2), 2, t2, gu)
                        scale_tokens(g_up + KF - 2, gu, 2)
                    split_lo(down_base + j, down_base + j)
                    if j == 0:
                        gate_hidden(KF - 2, n_h)
                    if j == 1:
                        hidden_lo(KF - 2, n_h)
                add_halves(g_up + KF - 1, 2 * ((KF - 1) % 2), 2, t2, gu)
                scale_tokens(g_up + KF - 1, gu, 2)
                gate_hidden(KF - 1, n_h)
                hidden_lo(KF - 1, n_h)
                for d, s in tiles(dve, KD, 4, 4):
                    for j in range(DOWN_PIECES):
                        if not (s == 0 and j < 4):
                            split_lo(d * DOWN_PIECES + (down_base + j), down_base + s * DOWN_PIECES + j)
                        if s >= 1 and j == 3:
                            add_halves(d + (g_down - 1), (s + 1) % 4, 1, t2[:, 0:1, :], f[:, bass.ds(d - 1, 1), :])
                        if s >= 1 and j == 4:
                            add_square(d - 1, s - 1, n_sq)
                        if s == 2 and j == 1:
                            beside_down()

            def after_down(nxt, m):
                if nxt is not None:
                    for j in range(3):
                        split_lo(nxt + j, nxt + j)
                inverse(m, post_scale[:, :])

            v.memset(ones[:, :], 1.0).then_inc(ones_set, 1)

            lam = param[:, C_LAM:C_LAM + REC_TILES]
            z, z2, series = soft[:, 3, :], soft[:, 4, :], soft[:, 5, :]
            steps = [0]

            def chained(ins):
                ins.then_inc(soft_step, 1)
                steps[0] += 1
                dve.wait_ge(soft_step, steps[0])

            def softplus():
                dve.wait_ge(soft_act, 2)
                e = soft[:, 1, :]
                chained(v.tensor_scalar(soft[:, 2, :], e, 2.0, None, ALU.add))
                chained(v.reciprocal(soft[:, 6, :], soft[:, 2, :]))
                chained(v.tensor_tensor(z, e, soft[:, 6, :], ALU.mult))
                chained(v.tensor_tensor(z2, z, z, ALU.mult))
                chained(v.tensor_scalar(series, z2, 1.0 / 15, None, ALU.mult))
                for odd in (13, 11, 9, 7, 5, 3):
                    chained(v.scalar_tensor_tensor(series, series, 1.0 / odd, z2, ALU.add, ALU.mult))
                chained(v.scalar_tensor_tensor(series, series, 1.0, z, ALU.add, ALU.mult))
                chained(v.tensor_scalar(rec_const[:, 0:2, :].rearrange("p a t -> p (a t)"),
                                        param[:, C_BA:C_BX + REC_TILES], 0.5, None, ALU.mult))
                chained(v.tensor_scalar(soft[:, 7, :], lam, -2.0, 0.0, ALU.mult, ALU.max))
                chained(v.scalar_tensor_tensor(rec_const[:, 2, :], series, 4.0, soft[:, 7, :], ALU.mult, ALU.add))

            for k in range(KD):
                if k % 4 == 0:
                    split_lo(k // 4, k // 4)
                    if k == 0:
                        dve.wait_ge(params_loaded, 16)
                    dve.wait_ge(x_loaded[k // 4], 16)
                operand_lo(k, C_FFN1_PRE, 0)
            ffn(UP1, DOWN1, G_UP1, G_DOWN1, 0, 0, 0, softplus)
            after_down(REC, 1)

            def beside_update(k):
                if k in UPDATE_LO:
                    split_lo(REC + UPDATE_LO[k], REC + UPDATE_LO[k])

            update_x(1, 0, C_MIX_PRE, KD, beside_update)
            v.memset(xg[:, :, 0:4], 0.0).then_inc(pads_zero, 1)

            def conv_rest(n, s):
                dve.wait_ge(conv0, n + 1)
                for tap in (1, 2, 3):
                    if tap > 1:
                        dve.wait_ge(conv_step, n * 2 + (tap - 1))
                    ins = v.scalar_tensor_tensor(conv[:, s % 2, :], xg[:, 0, 1 + tap:T + 1 + tap],
                                                 param[:, bass.ds(n + (C_CONV_W + REC_TILES * tap), 1)],
                                                 conv[:, s % 2, :], ALU.mult, ALU.add)
                    ins.then_inc(conv_step if tap < 3 else conv_done, 1)

            def recurrence_inputs(n, s):
                tile = lambda a: a[:, bass.ds(n, 1), :].rearrange("p a t -> p (a t)")
                dve.wait_ge(gate_tanh, n * 3 + 3)
                v.tensor_scalar(q_rec[:, :], tile(tanh_la), 1.0, None, ALU.add).then_inc(rec_step, 1)
                v.scalar_tensor_tensor(tile(gated_in), gate_t[:, 1, :], 1.0, conv[:, s % 2, :], ALU.add, ALU.mult)\
                    .then_inc(rec_step, 1)
                dve.wait_ge(rec_step, n * 5 + 1)
                v.reciprocal(q_rec[:, :], q_rec[:, :]).then_inc(rec_step, 1)
                dve.wait_ge(rec_step, n * 5 + 3)
                v.tensor_scalar(tile(decay), q_rec[:, :], 2.0, -1.0, ALU.mult, ALU.add).then_inc(rec_step, 1)
                v.tensor_tensor(tile(gated_in), tile(gated_in), q_rec[:, :], ALU.mult).then_inc(rec_step, 1)

            def rec_stages(n, s, j):
                if j == 0 and 2 <= s < REC_TILES + 2:
                    conv_rest(n - 2, s - 2)
                if j == 3 and 3 <= s < REC_TILES + 3:
                    recurrence_inputs(n - 3, s - 3)

            def rec_evacuate(n, s):
                if s >= 1:
                    dve.wait_ge(gelu_done, n)
                    dve.wait_ge(conv_done, n)
                add_halves(n + G_REC, 2 * ((s + 1) % 2), 2, t2, xg[:, :, 4:T + 4])
                if s >= 1:
                    scale_tokens(n + G_REC, xg[:, :, 4:T + 4], 2)

            for n, s in tiles(dve, REC_TILES, 4, 2):
                for j in range(4):
                    if j == 0 and s >= 2:
                        rec_evacuate(n - 2, s - 2)
                    if s and not (s == 1 and j == 0):
                        split_lo(n * 4 + (REC + j), REC + 4 * s + j)
                    if s != 2:
                        rec_stages(n, s, j)
                if s == 2:
                    pre_inverse(2)
                    scale_tokens(G_REC, xg[:, :, 4:T + 4], 2)
                    rec_stages(2, 2, 0)

            def rotate(h):
                qk = qkv[0:32, 0:2, :]
                dve.wait_ge(scaled, KF + REC_TILES + h + 1)
                v.stream_shuffle(rope_tmp[:, :, :], qk, list(range(16, 32)) + list(range(16))).then_inc(rope_step, 1)
                dve.wait_ge(rope_step, 4 * h + 1)
                v.tensor_tensor(rope_tmp[:, :, :], rope_tmp[:, :, :], rope_t[:, 1:2, :].to_broadcast([32, 2, T]),
                                ALU.mult).then_inc(rope_step, 1)
                v.tensor_tensor(qk, qk, rope_t[:, 0:1, :].to_broadcast([32, 2, T]), ALU.mult).then_inc(rope_step, 1)
                dve.wait_ge(rope_step, 4 * h + 3)
                v.tensor_tensor(qk, qk, rope_tmp[:, :, :], ALU.add).then_inc(rope_step, 1)

            def softmax_max(h):
                dve.wait_ge(scored, h + 1)
                if h >= 1:
                    dve.wait_ge(p_turned, h)
                v.tensor_tensor(prob, banks[:, 6, 0:3 * P], mask[:, :], ALU.add).then_inc(softmax_step, 1)
                dve.wait_ge(softmax_step, 4 * h + 1)
                v.tensor_reduce(stat[:, 0:1], prob[:, 0:P], AX.X, ALU.max).then_inc(softmax_step, 1)
                v.tensor_reduce(stat[:, 1:2], prob[:, P:3 * P], AX.X, ALU.max).then_inc(softmax_step, 1)
                dve.wait_ge(softmax_step, 4 * h + 3)
                v.tensor_scalar(stat[:, 2:4], stat[:, 0:2], -(P ** -0.5), None, ALU.mult).then_inc(softmax_step, 1)

            def softmax_divide(h):
                dve.wait_ge(exp_done, 2 * h + 2)
                v.reciprocal(stat[:, 6:8], stat[:, 4:6]).then_inc(rec_den, 1)
                dve.wait_ge(rec_den, h + 1)
                v.tensor_scalar(prob[:, 0:P], prob[:, 0:P], stat[:, 6:7], None, ALU.mult).then_inc(p_ready, 1)
                v.tensor_scalar(prob[:, P:3 * P], prob[:, P:3 * P], stat[:, 7:8], None, ALU.mult).then_inc(p_ready, 1)

            def scan(j):
                dve.wait_ge(u_done, j + 1)
                v.tensor_tensor_scan(decay[:, j, :], decay[:, j, :], gated_in[:, j, :], 0.0, ALU.mult, ALU.add)\
                    .then_inc(scan_step, 1)
                dve.wait_ge(scan_step, j + 1)
                dve.wait_ge(gelu_done, REC_TILES)
                v.scalar_tensor_tensor(gated_in[:, j, :], decay[:, j, :], 0.5, gelu[:, j, :], ALU.mult, ALU.mult)\
                    .then_inc(rec_done, 1)

            def att_evacuate(h):
                if h >= 1:
                    dve.wait_ge(v_turned, h)
                    dve.wait_ge(scored, h)
                add_halves(G_ATT + h, 3 * ((h + 1) % 2), 3, t3, qkv[:, :, :])
                scale_tokens(G_ATT + h, qkv[:, :, :], 3)
                rotate(h)

            def out_rec(g, j):
                add_halves(g * 8 + (G_OUT + j), OUT_BANKS[j], 1, t2[:, 0:1, :], f[:, bass.ds(g * 4 + j, 1), :])

            def out_att(g, s, j):
                if s >= 1 or j >= 1:
                    dve.wait_ge(halves_added, g * 4 + j)
                add_halves(g * 8 + (G_OUT + 4 + j), OUT_BANKS[j], 1, t2[:, 0:1, :], t2[:, 1:2, :])
                dve.wait_ge(evacuated, g * 8 + (G_OUT + 5 + j))
                v.tensor_tensor(t2[:, 1, :], t2[:, 1, :], half_norms[:, 1, :], ALU.mult).then_inc(att_scaled, 1)

            def add_out(g, j):
                dve.wait_ge(rec_scaled, g * 4 + (j + 1))
                dve.wait_ge(att_scaled, g * 4 + (j + 1))
                tile = f[:, bass.ds(g * 4 + j, 1), :]
                v.tensor_tensor(tile, tile, t2[:, 1:2, :], ALU.add).then_inc(halves_added, 1)

            dve.wait_ge(mixer_loaded, 3 * 16)
            for h in range(HEADS + 1):
                base = ATT + 6 * h
                for j in range(6 if h < HEADS else 4):
                    if h < 2 and j == 0:
                        rec_evacuate(REC_TILES - 2 + h, REC_TILES - 2 + h)
                    if h == HEADS and j == 3:
                        att_evacuate(h - 1)
                    split_lo(base + j, base + j)
                    if h < 2 and j == 0 or h == 0 and j == 3:
                        rec_stages(REC_TILES + h, REC_TILES + h, j)
                    if h < 2 and j == 5:
                        recurrence_inputs(REC_TILES - 2 + h, REC_TILES - 2 + h)
                    if h >= 2 and j == (1 if h < HEADS else 0):
                        softmax_max(h - 2)
                    if h == HEADS and j == 2:
                        softmax_divide(h - 2)
                    if 2 <= h < HEADS and j == 3:
                        softmax_divide(h - 2)
                    if 1 <= h < HEADS and j == 3:
                        att_evacuate(h - 1)
                    if 3 <= h <= 6 and j in (2, 4):
                        scan(2 * (h - 3) + (j == 4))

            softmax_max(HEADS - 1)
            split_lo(OUT + 4, OUT + 4)
            out_rec(0, 0)
            softmax_divide(HEADS - 1)
            out_rec(0, 1)
            split_lo(OUT + 5, OUT + 5)
            out_rec(0, 2)
            split_lo(OUT + 6, OUT + 6)
            inverse(3, half_norms[:, 0, :])
            out_rec(0, 3)
            split_lo(OUT + 7, OUT + 7)

            for g, s in tiles(dve, KD // 4 - 1, 1, 1):
                for j in range(4):
                    if s == 0 and j == 0:
                        split_lo(OUT + 8, OUT + 8)
                        inverse(4, half_norms[:, 1, :])
                        dve.wait_ge(norm_ready, 5)
                    out_att(g, s, j)
                    add_out(g, j)
                    if s or j:
                        split_lo(g * 8 + (OUT + 8 + j), OUT + 8 + s * 8 + j)
                    add_square(g * 4 + j, s * 4 + j, KD - 1)
                for j in range(4):
                    out_rec(g + 1, j)
                    split_lo(g * 8 + (OUT + 12 + j), OUT + 12 + s * 8 + j)
            g = KD // 4 - 1
            for j in range(3):
                out_att(g, g, j)
                add_out(g, j)
                if j < 2:
                    split_lo(UP2 + j, UP2 + j)
                    add_square(KD - 4 + j, KD - 4 + j, KD - 1)
            dve.wait_ge(piece_used, UP2)
            v.tensor_tensor(t2[:, 0, :], banks[:, OUT_BANKS[3], 0:T], half_norms[:, 1, :], ALU.mult)\
                .then_inc(evacuated, 1)
            dve.wait_ge(evacuated, G_OUT + 2 * KD)
            dve.wait_ge(rec_scaled, KD)
            v.tensor_tensor(f[:, KD - 1, :], f[:, KD - 1, :], t2[:, 0, :], ALU.add).then_inc(halves_added, 1)
            split_lo(UP2 + 2, UP2 + 2)
            inverse(5, post_scale[:, :])
            update_x(5, 1, C_FFN2_PRE, 2 * KD,
                     lambda k: split_lo(UP2 + UPDATE_LO[k], UP2 + UPDATE_LO[k]) if k in UPDATE_LO else None)
            ffn(UP2, DOWN2, G_UP2, G_DOWN2, 6, KF, N_SQ[2])
            after_down(None, 7)
            update_x(7, 2, None, None)

        @block.gpsimd
        def _(pool):
            p = nc.gpsimd

            def add_f(n):
                for k in range(KD):
                    if n == 2 and by_vector(k):
                        continue
                    pool.wait_ge(f_scaled, scalings(n, k))
                    p.tensor_tensor(xs[:, k, :], xs[:, k, :], f[:, k, :], ALU.add).then_inc(x_new, 1)

            def tree_sum(n):
                spans = [(4, 4), (8, 4), (12, 4), (2, 2), (1, 1)]
                for step, (start, width) in enumerate(spans):
                    pool.wait_ge(x_squared, 4 * n + min(step + 2, 4))
                    if step:
                        pool.wait_ge(tree, 5 * n + step)
                    p.tensor_tensor(squares[:, 0:width, :], squares[:, 0:width, :],
                                    squares[:, start:start + width, :], ALU.add).then_inc(tree, 1)

            tree_sum(0)
            add_f(0)
            pool.wait_ge(x_new, KD)
            p.memset(gate_w[:, :, :, :], 0.0).then_inc(pads_zero, 1)
            tree_sum(1)
            pool.wait_ge(gates_loaded, 4 * 16)
            for n in range(REC_TILES):
                if n >= 2:
                    pool.wait_ge(gates_done, n - 1)
                p.tensor_copy(gate_w2[:, n % 2, :, :], gate_w[:, n, :, :]).then_inc(gatew_now, 1)
                pool.wait_ge(gr_squared, n + 1)
                pool.wait_ge(scaled, KF + n + 1)
                gr = xg[:, 1, 4:T + 4]
                p.tensor_scalar(gelu_tmp[:, :], gelu_tmp[:, :], GELU_C, 1.0, ALU.mult, ALU.add).then_inc(gelu_step, 1)
                pool.wait_ge(gelu_step, 2 * n + 1)
                p.tensor_tensor(gelu_tmp[:, :], gelu_tmp[:, :], gr, ALU.mult).then_inc(gelu_step, 1)
                pool.wait_ge(gelu_th, n + 1)
                p.tensor_tensor(gelu[:, n, :], gelu_tmp[:, :], gr, ALU.mult).then_inc(gelu_mul, 1)
                pool.wait_ge(gelu_mul, n + 1)
                p.tensor_tensor(gelu[:, n, :], gelu[:, n, :], gr, ALU.add).then_inc(gelu_done, 1)
            pool.wait_ge(root_t, 1)
            pool.wait_ge(rec_step, 5 * REC_TILES)

            def u(j):
                p.tensor_tensor(gated_in[:, j, :], gated_in[:, j, :], tanh_la[:, j, :], ALU.mult).then_inc(u_done, 1)

            def add_rec_square(j):
                pool.wait_ge(rec_sqd, j + 1)
                if j == 0:
                    p.tensor_copy(post_scale[:, :], rec_sq[:, :]).then_inc(rec_sum, 1)
                else:
                    pool.wait_ge(rec_sum, j)
                    p.tensor_tensor(post_scale[:, :], post_scale[:, :], rec_sq[:, :], ALU.add).then_inc(rec_sum, 1)

            def add_att_square(h):
                pool.wait_ge(att_sqd, h + 1)
                if h == 0:
                    p.tensor_copy(att_total[:, :], gelu_tmp[:, :]).then_inc(att_sum, 1)
                elif h < HEADS - 1:
                    pool.wait_ge(att_sum, h)
                    p.tensor_tensor(att_total[:, :], att_total[:, :], gelu_tmp[:, :], ALU.add).then_inc(att_sum, 1)
                else:
                    pool.wait_ge(att_sum, h)
                    pool.wait_ge(scaled, KF + REC_TILES + HEADS)
                    p.tensor_tensor(pre_scale[:, :], att_total[:, :], gelu_tmp[:, :], ALU.add).then_inc(att_sum, 1)

            def operand_rest(h, k, gained, made, lo):
                pool.wait_ge(made, 2 * h + 2)
                p.tensor_tensor(merged[:, k, T:2 * T], gained[:, h, :], merged[:, k, 0:T].bitcast(F32),
                                ALU.subtract).then_inc(lo, 1)

            for j in range(2):
                u(j)
            for h in range(3, 8):
                add_att_square(h - 3)
                operand_rest(h - 3, PIECE + h - 3, att, att_made, att_lo)
                if h < 6:
                    u(2 * (h - 2))
                    u(2 * (h - 2) + 1)
                for j in (2 * (h - 4) + 1, 2 * (h - 3)):
                    if 0 <= j < REC_TILES:
                        add_rec_square(j)
                        operand_rest(j, j, gelu, rec_made, rec_lo)
            for h in range(5, HEADS):
                if h < HEADS - 1:
                    add_att_square(h)
                operand_rest(h, PIECE + h, att, att_made, att_lo)
            add_att_square(HEADS - 1)
            pool.wait_ge(norm_ready, 4)
            for k in range(KD):
                pool.wait_ge(evacuated, G_OUT + 8 * (k // 4) + k % 4 + 1)
                p.tensor_tensor(f[:, k, :], f[:, k, :], half_norms[:, 0, :], ALU.mult).then_inc(rec_scaled, 1)
            add_f(1)
            tree_sum(2)
            add_f(2)


def weight_tiles(w, order):
    k, n = w.shape
    tiled = w.reshape(k // P, P, n // P, P).transpose(2, 1, 0, 3)
    return np.ascontiguousarray(tiled[order]).reshape(n // P, P, k)


def channels(vector):
    return vector.reshape(-1, P).T


def kernel(x, ffn1_pre_g, ffn1_w_gate_up, ffn1_w_down, ffn1_post_g, mix_pre_g, w_in, conv_w, conv_b,
           rg_w_a, rg_b_a, rg_w_x, rg_b_x, rg_lambda, attn_out_g, rec_out_g, w_out, mix_post_g,
           ffn2_pre_g, ffn2_w_gate_up, ffn2_w_down, ffn2_post_g):
    import concourse.bacc as bacc
    from concourse.bass_utils import run_bass_kernel_spmd

    n = lambda a: np.asarray(a)
    pairs = [i for t in range(KF) for i in (t, KF + t)]
    rec_order = [i for t in range(8) for i in (24 + t, 32 + t)]
    att_order = [i for t in range(8) for i in (t, 8 + t, 16 + t)]
    w_in = n(w_in)[0]
    in_tiles = weight_tiles(w_in, list(range(40)))
    w_out_rec_first = np.concatenate([n(w_out)[0][D // 2:], n(w_out)[0][:D // 2]])
    plain = list(range(KD))

    eps = np.full((P, 2), EPS, np.float32)
    eps[:, 1] = 4 * EPS
    columns = [channels(n(a)[0]) for a in (
        ffn1_pre_g, ffn1_post_g, mix_pre_g, rec_out_g, attn_out_g, mix_post_g, ffn2_pre_g, ffn2_post_g,
        conv_w, conv_b, rg_b_a, rg_b_x, rg_lambda)] + [eps]
    gates = np.stack([n(g)[0].reshape(8, 2, 64, 64).transpose(1, 2, 0, 3) for g in (rg_w_a, rg_w_x)])

    rot = 32
    inv_freq = np.float32(500000.0) ** (-np.arange(0, rot, 2, dtype=np.float32) / np.float32(rot))
    angle = (np.arange(T, dtype=np.float32)[:, None] * inv_freq.astype(np.float32)[None, :]).T
    cos, sin = np.cos(angle).astype(np.float32), np.sin(angle).astype(np.float32)
    rope = np.stack([np.concatenate([cos, cos]), np.concatenate([-sin, sin])], axis=1)
    causal = np.where(np.arange(P)[None, :] <= np.arange(P)[:, None], 0.0, MASKED).astype(np.float32)
    consts = np.concatenate([causal, causal, np.zeros((P, P), np.float32), np.eye(P, dtype=np.float32)], axis=1)

    ins = {
        "x_in": n(x)[0].reshape(T, KD, P).transpose(2, 1, 0),
        "up1_w": weight_tiles(n(ffn1_w_gate_up)[0], pairs),
        "down1_w": weight_tiles(n(ffn1_w_down)[0], plain),
        "rec_w": in_tiles[rec_order],
        "att_w": in_tiles[att_order],
        "out_w": weight_tiles(w_out_rec_first, plain),
        "up2_w": weight_tiles(n(ffn2_w_gate_up)[0], pairs),
        "down2_w": weight_tiles(n(ffn2_w_down)[0], plain),
        "params": np.concatenate(columns, axis=1),
        "gates": gates,
        "rope": rope,
        "consts": consts,
    }
    ins = {name: np.ascontiguousarray(a) for name, a in ins.items()}
    nc = bacc.Bacc("TRN2", target_bir_lowering=False, num_devices=1)
    args = [nc.dram_tensor(name, a.shape, F32, kind="ExternalInput").ap() for name, a in ins.items()]
    y = nc.dram_tensor("y_out", (P, KD, T), F32, kind="ExternalOutput").ap()
    layer(nc, *args, y)
    got = run_bass_kernel_spmd(nc, [ins], core_ids=[0]).results[0]["y_out"]
    return np.ascontiguousarray(got.transpose(2, 1, 0)).reshape(1, T, D)
```
